# Optimizing a Trainium2 kernel written in Bass

```python
import jax, jax.numpy as jnp
from jax import lax
import numpy as np

D_MODEL = 1024
BATCH = 1
SEQ = 1024
DEPTH = 1

D_POOL = D_MODEL
POOL_WINDOWS = (2, 4, 8, 16)
N_POOL_GROUPS = len(POOL_WINDOWS)
POOL_GROUP = D_POOL // N_POOL_GROUPS
D_REC = D_MODEL
HEAD_DIM = 128
N_REC_HEADS = D_REC // HEAD_DIM
CHUNK = 64
D_MIX = D_POOL + D_REC
D_IN_PROJ = 2 * D_POOL + 4 * D_REC
EPS = 1e-6

kernel_name = "hybrid_pool_hgrn2_parallel_heads"

def rmsnorm(x, g):
    xf = x.astype(jnp.float32)
    y = xf * lax.rsqrt(jnp.mean(xf * xf, axis=-1, keepdims=True) + EPS)
    return y.astype(x.dtype) * g

def causal_multiscale_pool(u, pool_w, pool_scale):
    B, T, _ = u.shape
    ug = u.reshape(B, T, N_POOL_GROUPS, POOL_GROUP).astype(jnp.float32)
    cs0 = jnp.pad(jnp.cumsum(ug, axis=1), ((0, 0), (1, 0), (0, 0), (0, 0)))
    pos = jnp.arange(T, dtype=jnp.float32)
    pooled = []
    for gi, w in enumerate(POOL_WINDOWS):
        c = cs0[:, :, gi]
        hi = c[:, 1:]
        lo = jnp.pad(c[:, : T + 1 - w], ((0, 0), (w - 1, 0), (0, 0)))
        count = jnp.minimum(pos + 1.0, float(w))[None, :, None]
        pooled.append((hi - lo) / count)
    pooled = jnp.stack(pooled, axis=2)
    mixed = jnp.einsum('btgc,gcd->btgd', pooled - ug, pool_w.astype(jnp.float32))
    return mixed.reshape(B, T, D_POOL).astype(u.dtype) * pool_scale

def hgrn2_chunked(q, k, v, log_f):
    B, H, T, Dk = q.shape
    Dv = v.shape[-1]
    n = T // CHUNK

    def to_chunks(a):
        return a.reshape(B, H, n, CHUNK, a.shape[-1]).transpose(2, 0, 1, 3, 4)

    qc, kc, vc, gc = to_chunks(q), to_chunks(k), to_chunks(v), to_chunks(log_f)
    causal = jnp.tril(jnp.ones((CHUNK, CHUNK), dtype=bool))[:, :, None]

    def step(S, inp):
        qb, kb, vb, gb = inp
        G = jnp.cumsum(gb, axis=2)
        diff = G[:, :, :, None, :] - G[:, :, None, :, :]
        decay = jnp.exp(jnp.where(causal, diff, -jnp.inf))
        A = jnp.einsum('bhtd,bhsd,bhtsd->bhts', qb, kb, decay)
        o = (jnp.einsum('bhts,bhsv->bhtv', A, vb)
             + jnp.einsum('bhtd,bhdv->bhtv', qb * jnp.exp(G), S))
        G_last = G[:, :, -1]
        k_dec = kb * jnp.exp(G_last[:, :, None, :] - G)
        S = jnp.exp(G_last)[..., None] * S + jnp.einsum('bhsd,bhsv->bhdv', k_dec, vb)
        return S, o

    S0 = jnp.zeros((B, H, Dk, Dv), jnp.float32)
    _, o = lax.scan(step, S0, (qc, kc, vc, gc))
    return o.transpose(1, 2, 0, 3, 4).reshape(B, H, T, Dv)

def hybrid_layer(x, norm_g, w_in, pool_w, pool_scale, lb, rec_norm_g, w_out):
    B, T, _ = x.shape
    h = rmsnorm(x, norm_g)
    proj = jnp.einsum('btd,de->bte', h, w_in)
    o = 0
    pool_in = proj[..., o:o + D_POOL]; o += D_POOL
    pool_gate = proj[..., o:o + D_POOL]; o += D_POOL
    q = proj[..., o:o + D_REC]; o += D_REC
    f_logit = proj[..., o:o + D_REC]; o += D_REC
    i_in = proj[..., o:o + D_REC]; o += D_REC
    rec_gate = proj[..., o:o + D_REC]

    y_pool = causal_multiscale_pool(pool_in, pool_w, pool_scale) * jax.nn.silu(pool_gate)

    def heads(a):
        return a.astype(jnp.float32).reshape(B, T, N_REC_HEADS, HEAD_DIM).transpose(0, 2, 1, 3)

    f = lb + (1.0 - lb) * jax.nn.sigmoid(f_logit.astype(jnp.float32))
    rec = hgrn2_chunked(heads(jax.nn.silu(q)), heads(1.0 - f), heads(i_in), heads(jnp.log(f)))
    rec = rec.transpose(0, 2, 1, 3)
    rec = rec * lax.rsqrt(jnp.mean(rec * rec, axis=-1, keepdims=True) + EPS)
    rec = rec.reshape(B, T, D_REC).astype(x.dtype) * rec_norm_g
    y_rec = rec * jax.nn.silu(rec_gate)

    y = jnp.concatenate([y_pool, y_rec], axis=-1)
    return x + jnp.einsum('bte,ed->btd', y, w_out)

def setup_inputs(seed: int = 0) -> dict:
    key = jax.random.key(seed)
    ks = jax.random.split(key, 9)
    f32 = jnp.float32
    return {
        "x": jax.random.normal(ks[0], (BATCH, SEQ, D_MODEL), f32),
        "norm1_g": 1.0 + 0.02 * jax.random.normal(ks[1], (DEPTH, D_MODEL), f32),
        "w_in": jax.random.normal(ks[2], (DEPTH, D_MODEL, D_IN_PROJ), f32) * D_MODEL ** -0.5,
        "pool_w": jax.random.normal(ks[3], (DEPTH, N_POOL_GROUPS, POOL_GROUP, POOL_GROUP), f32) * POOL_GROUP ** -0.5,
        "pool_scale": 1.0 + 0.02 * jax.random.normal(ks[4], (DEPTH, D_POOL), f32),
        "lb_logits": 0.5 * jax.random.normal(ks[5], (DEPTH + 1, D_REC), f32),
        "rec_norm_g": 1.0 + 0.02 * jax.random.normal(ks[6], (DEPTH, D_REC), f32),
        "w_out": jax.random.normal(ks[7], (DEPTH, D_MIX, D_MODEL), f32) * D_MIX ** -0.5,
        "final_norm_g": 1.0 + 0.02 * jax.random.normal(ks[8], (D_MODEL,), f32),
    }

def reference(x, norm1_g, w_in, pool_w, pool_scale, lb_logits, rec_norm_g, w_out, final_norm_g):
    lb_all = jnp.cumsum(jax.nn.softmax(lb_logits.astype(jnp.float32), axis=0), axis=0)
    for layer in range(DEPTH):
        x = hybrid_layer(x, norm1_g[layer], w_in[layer], pool_w[layer], pool_scale[layer],
                         lb_all[layer], rec_norm_g[layer], w_out[layer])
    return rmsnorm(x, final_norm_g)


_drawn_inputs = setup_inputs


def setup_inputs(seed=0):
    import zlib

    import numpy as np

    out = dict(_drawn_inputs(seed))
    spreads = {}
    factors = {'norm1_g': 3.745,
     'pool_scale': 23.983,
     'rec_norm_g': 60.264,
     'final_norm_g': 8.95,
     'lb_logits': 3.698}
    for name, (base, spread) in spreads.items():
        noise = np.random.default_rng([zlib.crc32(name.encode()), seed]).standard_normal(out[name].shape)
        drawn = base * np.exp(spread * noise) if base else spread * noise
        out[name] = __import__('jax').numpy.asarray(drawn.astype(out[name].dtype))
    for name, factor in factors.items():
        out[name] = (out[name] * factor).astype(out[name].dtype)
    return out
```

```python
import concourse.bass as bass
from concourse import mybir
from contextlib import ExitStack


def hybrid_pool_hgrn2_kernel(nc, x, norm1_g, w_in, pool_w, pool_scale, lb_logits,
                             rec_norm_g, w_out, final_norm_g, out):
    f32 = mybir.dt.float32
    f32r = mybir.dt.float32r
    u32 = mybir.dt.uint32
    ALU = mybir.AluOpType
    ACT = mybir.ActivationFunctionType
    AX = mybir.AxisListType
    ds = bass.ds

    P = 128
    T, D = x.shape[1], x.shape[2]
    KT = D // P
    TT = T // P
    HALF = 512
    NH = T // HALF
    C = P
    HC = C // 2
    HEADS = D // P
    GROUPS = pool_w.shape[1]
    PT = D // GROUPS // P
    EPS = 1e-6
    PAD = 16
    BLOCKS = HEADS + GROUPS
    UNITS = 4 * BLOCKS
    SLOTS = HEADS + PT * GROUPS
    OG = 2
    OT = TT // OG

    POOL_IN, POOL_GATE, QC, FC, VC, GC = (k * D for k in range(6))

    w_in_v = w_in[0].rearrange("(k p) n -> p k n", p=P)
    w_out_v = w_out[0].rearrange("(s p) n -> p s n", p=P)
    pool_w_v = pool_w[0].rearrange("g (c p) n -> g p c n", p=P)
    x_v = x[0].rearrange("(t p) d -> t p d", p=P)
    out_v = out[0].rearrange("(t p) d -> t p d", p=P)

    ctx = ExitStack()
    with ctx:
        def sb(name, shape, dt=f32):
            return ctx.enter_context(nc.sbuf_tensor(name, shape, dt))

        def sem(name):
            return ctx.enter_context(nc.semaphore(name))

        h_hi = sb("h_hi", [P, KT, T], f32r)
        h_lo = sb("h_lo", [P, KT, T], f32r)
        Y = sb("Y", [P, SLOTS, T])
        w_raw = sb("w_raw", [P, 2, KT * P])
        w_hi = sb("w_hi", [P, 2, KT * P], f32r)
        w_lo = sb("w_lo", [P, 2, KT * P], f32r)
        m_hi = sb("m_hi", [P, T + 2 * PT * P], f32r)
        m_lo = sb("m_lo", [P, T + 2 * PT * P], f32r)
        Qp = sb("Qp", [P, PAD + T])
        Kp = sb("Kp", [P, PAD + T])
        Fp = sb("Fp", [P, PAD + T])
        Gp = sb("Gp", [P, PAD + T])
        Q, K, F, G = (b[:, PAD:PAD + T] for b in (Qp, Kp, Fp, Gp))
        V = sb("V", [P, T])
        X1 = sb("X1", [P, T])
        AT = sb("AT", [P, TT, C])
        S = sb("S", [P, T])
        GATE = sb("GATE", [P, T])
        SIG = sb("SIG", [P, T])

        ident = sb("ident", [P, P])
        mean_w = sb("mean_w", [P, P])
        masks = sb("masks", [P, 6, HC])
        rcount = sb("rcount", [P, PAD])
        fix = sb("fix", [P, PAD])
        eps = sb("eps", [P, 1])
        lbl = sb("lbl", [P, 2, HEADS])
        lbm = sb("lbm", [P, HEADS])
        lb = sb("lb", [P, HEADS])
        omlb = sb("omlb", [P, HEADS])
        rg = sb("rg", [P, HEADS])
        psc = sb("psc", [P, HEADS])
        ss = sb("ss", [P, TT])
        rms = sb("rms", [P, TT])
        rin = sb("rin", [P, TT])

        PJ = [ctx.enter_context(nc.psum_tensor(f"PJ{i}", [P, T], f32)) for i in range(2)]
        LV = ctx.enter_context(nc.psum_tensor("LV", [P, T], f32))
        R = ctx.enter_context(nc.psum_tensor("R", [P, T], f32))
        BANKS = [PJ[0], PJ[1], LV, R]

        x_loaded = [sem(f"x_loaded{t}") for t in range(TT)]
        params_loaded = sem("params_loaded")
        grow_loaded = sem("grow_loaded")
        w_loaded = [sem(f"w_loaded{i}") for i in range(2)]
        pw_loaded = sem("pw_loaded")
        xres_loaded = [sem(f"xres_loaded{t}") for t in range(OT)]
        gfin_loaded = sem("gfin_loaded")
        out_stored = [sem(f"out_stored{t}") for t in range(OT)]
        consts = sem("consts")
        const_step = sem("const_step")
        ss_ready = sem("ss_ready")
        rms_ready = sem("rms_ready")
        rin_ready = sem("rin_ready")
        xn_ready = sem("xn_ready")
        xT_ready = sem("xT_ready")
        hhi_ready = sem("hhi_ready")
        hlo_ready = sem("hlo_ready")
        lb_step = sem("lb_step")
        lb_exp = sem("lb_exp")
        whi_ready = sem("whi_ready")
        wlo_ready = sem("wlo_ready")
        unit_done = sem("unit_done")
        fsig_ready = sem("fsig_ready")
        qsig_ready = sem("qsig_ready")
        gsig_ready = sem("gsig_ready")
        vT_ready = sem("vT_ready")
        v_ready = sem("v_ready")
        kd_ready = sem("kd_ready")
        sq_ready = sem("sq_ready")
        orms_ready = sem("orms_ready")
        at_act = sem("at_act")
        at_dve = sem("at_dve")
        fk_ready = sem("fk_ready")
        q_ready = sem("q_ready")
        tree = sem("tree")
        state = sem("state")
        gate_ready = sem("gate_ready")
        oy_ready = sem("oy_ready")
        orin_ready = sem("orin_ready")
        y_ready = sem("y_ready")
        lvl_done = sem("lvl_done")
        vtr_done = sem("vtr_done")
        kdtr_done = sem("kdtr_done")
        kv_done = sem("kv_done")
        o_done = sem("o_done")
        mean_done = sem("mean_done")
        u_ready = sem("u_ready")
        pool_step = sem("pool_step")
        pool_dd = sem("pool_dd")
        dhi_ready = sem("dhi_ready")
        dlo_ready = sem("dlo_ready")
        pwhi_ready = sem("pwhi_ready")
        pwlo_ready = sem("pwlo_ready")
        psig_ready = sem("psig_ready")
        pgate_ready = sem("pgate_ready")
        mix_done = sem("mix_done")
        py_ready = sem("py_ready")
        yhi_ready = sem("yhi_ready")
        ylo_ready = sem("ylo_ready")
        tile_done = sem("tile_done")
        res_ready = sem("res_ready")
        fss_ready = sem("fss_ready")
        frms_ready = sem("frms_ready")
        frin_ready = sem("frin_ready")
        fin_ready = sem("fin_ready")

        LEVELS = [2, 4, 8, 16, 32, 64]
        LVLS = 2 + len(LEVELS)
        TS = 4 + 3 * len(LEVELS)
        AD, AA = 6, 3
        GOFF = {2: 0}
        for m in LEVELS:
            GOFF[2 * m] = GOFF[m] + T // m

        def seg_total(m):
            return F if m == 1 else G[:, GOFF[m]:GOFF[m] + T // m]

        def halves(b, m, which):
            return b.rearrange("p (n two m) -> p n two m", two=2, m=m)[:, :, which, :]

        def lv(j):
            return LV[:, (j % 2) * HALF:(j % 2 + 1) * HALF]

        block = ctx.enter_context(nc.Block())

        N_CONSTS = 1 + 5 + 3 + 4 + PAD
        RES = [AT[:].rearrange("p c t -> p (c t)"), GATE[:], S[:], SIG[:]]

        @block.gpsimd
        def _(pool):
            step = 0
            pool.memset(ident[:], 0.0).then_inc(const_step, 1)
            pool.memset(masks[:], 1.0).then_inc(const_step, 1)
            pool.wait_ge(const_step, 2)
            step = 2
            pool.affine_select(out=ident[:], in_=ident[:], compare_op=ALU.not_equal, fill=1.0, base=0,
                               pattern=[[-1, P]], channel_multiplier=1).then_inc(consts, 1)
            pool.affine_select(out=masks[:, 0, :], in_=masks[:, 0, :], compare_op=ALU.is_equal, fill=0.0,
                               base=0, pattern=[[-2, HC]], channel_multiplier=1).then_inc(const_step, 1)
            spans = [(1, 2, 2)] + [(1 + k, 2 * m, m) for k, m in enumerate(LEVELS[:4], 1)]
            for k, pair, width in spans:
                m = pair // 2
                mk = masks[:, k, :].rearrange("p (n m) -> p n m", m=m)
                pool.affine_select(out=mk, in_=mk, compare_op=ALU.is_ge, fill=0.0, base=0,
                                   pattern=[[-pair, HC // m], [0, m]], channel_multiplier=1).then_inc(const_step, 1)
            pool.wait_ge(const_step, 3 + len(spans))
            for k, pair, width in spans:
                m = pair // 2
                mk = masks[:, k, :].rearrange("p (n m) -> p n m", m=m)
                pool.affine_select(out=mk, in_=mk, compare_op=ALU.is_ge, fill=0.0, base=width - 1,
                                   pattern=[[pair, HC // m], [0, m]], channel_multiplier=-1).then_inc(consts, 1)
            pool.memset(mean_w[:], 1.0 / P).then_inc(consts, 1)
            pool.memset(eps[:], EPS).then_inc(consts, 1)
            pool.memset(AT[:], 0.0).then_inc(consts, 1)
            for b in (Qp, Kp, Fp, Gp):
                pool.memset(b[:, 0:PAD], 0.0).then_inc(consts, 1)
            for t in range(PAD):
                pool.memset(rcount[:, t:t + 1], 1.0 / (t + 1)).then_inc(consts, 1)
            for n in range(TT):
                pool.wait_ge(fin_ready, n + 1)
                pool.dma_start(out_v[n], RES[n % OT]).then_inc(out_stored[n % OT], 16)
            for t in range(OT):
                pool.wait_ge(out_stored[t], 16 * OG)


        @block.sync
        def _(sp):
            def load_unit(n, slot, src, first=False):
                if not first:
                    sp.wait_ge(wlo_ready, n - 1)
                sp.dma_start(w_raw[:, slot, :].rearrange("p (k n) -> p k n", n=P), src).then_inc(w_loaded[slot], 16)

            def load_head(i, first=False):
                for u, base in enumerate((FC, QC, VC, GC)):
                    load_unit(4 * i + u, u % 2, w_in_v[:, :, ds(base + i * P, P)], first and u < 2)

            def load_group(g):
                for u, (base, c) in enumerate(((POOL_IN, 0), (POOL_GATE, 0), (POOL_IN, 1), (POOL_GATE, 1))):
                    load_unit(4 * (HEADS + g) + u, u % 2, w_in_v[:, :, ds(base + c * P + g * (PT * P), P)])

            def load_pool_w(g):
                if isinstance(g, int) and g == 0:
                    sp.wait_ge(mean_done, HEADS)
                else:
                    sp.wait_ge(pwlo_ready, g)
                sp.dma_start(X1[:, 0:2 * PT * P].rearrange("p (a c n) -> p a c n", a=1, c=PT),
                             pool_w_v[ds(g, 1)].rearrange("a p c n -> p a c n")).then_inc(pw_loaded, 16)

            def load_out_pair(n, row):
                for u in range(2):
                    sp.wait_ge(wlo_ready, n + u - 1)
                    sp.dma_start(w_raw[:, u, :].rearrange("p (a n) -> p a n", a=1),
                                 w_out_v[:, ds(row + u, 1), :]).then_inc(w_loaded[u], 16)

            sp.dma_start(S[:], norm1_g.partition_broadcast(P)).then_inc(grow_loaded, 16)
            for t in range(TT):
                sp.dma_start(Y[:, SLOTS - TT + t, :], x_v[t]).then_inc(x_loaded[t], 16)
            load_head(0, first=True)
            with sp.Fori(1, HEADS) as i:
                load_head(i)
            load_group(0)
            load_pool_w(0)
            with sp.Fori(1, GROUPS) as g:
                load_group(g)
                load_pool_w(g)
            for o in range(OG):
                n0 = UNITS + SLOTS * o
                with sp.Fori(0, HEADS // 2) as j:
                    load_out_pair(n0 + 2 * j, (SLOTS - HEADS) + 2 * j)
                if o == 0:
                    sp.wait_ge(py_ready, PT * GROUPS)
                    sp.dma_start(V[:], final_norm_g.partition_broadcast(P)).then_inc(gfin_loaded, 16)
                for t, b in enumerate((Q, K, F, G)):
                    if o:
                        sp.wait_ge(res_ready, OT * (o - 1) + t + 1)
                    sp.dma_start(b, x_v[OT * o + t]).then_inc(xres_loaded[t], 16)
                with sp.Fori(0, (SLOTS - HEADS) // 2) as j:
                    load_out_pair(n0 + HEADS + 2 * j, 2 * j)

        @block.scalar
        def _(act):
            def split_hi(half_n, slot):
                act.wait_ge(w_loaded[slot], half_n * 16 + 16)
                if not (isinstance(half_n, int) and half_n == 0):
                    act.wait_ge(unit_done, half_n * 2 + slot - 1)
                act.activation(w_hi[:, slot, :], w_raw[:, slot, :], ACT.Copy).then_inc(whi_ready, 1)

            with nc.allow_non_contiguous_dma("parameters of 4 KB, transposed by the load"):
                act.dma_start(lbl[:], lb_logits.rearrange("l (h p) -> p l h", p=P)).then_inc(params_loaded, 16)
                act.dma_start(rg[:], rec_norm_g[0].rearrange("(h p) -> p h", p=P)).then_inc(params_loaded, 16)
                act.dma_start(psc[:], pool_scale[0].rearrange("(h p) -> p h", p=P)).then_inc(params_loaded, 16)

            act.wait_ge(lb_step, 3)
            act.activation(lbl[:], lbl[:], ACT.Exp).then_inc(lb_exp, 1)

            act.wait_ge(consts, N_CONSTS)
            for t in range(TT):
                act.wait_ge(x_loaded[t], 16)
                if t:
                    act.wait_ge(ss_ready, t)
                act.activation(X1[:], Y[:, SLOTS - TT + t, :], ACT.Square,
                               accum_out=ss[:, t:t + 1]).then_inc(ss_ready, 1)
                act.wait_ge(ss_ready, t + 1)
                act.activation(rms[:, t:t + 1], ss[:, t:t + 1], ACT.Sqrt, bias=eps[:, 0:1],
                               scale=1.0 / D).then_inc(rms_ready, 1)
                if t:
                    act.wait_ge(xT_ready, t)
                    act.activation(h_hi[:, :, (t - 1) * P:t * P],
                                   BANKS[(t - 1) % 4][:].rearrange("p (k n) -> p k n", n=P),
                                   ACT.Copy).then_inc(hhi_ready, 1)
                if t == TT - 2:
                    split_hi(0, 0)
            act.wait_ge(xT_ready, TT)
            act.activation(h_hi[:, :, (TT - 1) * P:T], BANKS[(TT - 1) % 4][:].rearrange("p (k n) -> p k n", n=P),
                           ACT.Copy).then_inc(hhi_ready, 1)

            def copy_level(h, j, m):
                act.wait_ge(lvl_done, LVLS * h + j + 1)
                act.wait_ge(at_dve, AD * h + AD)
                for n in range(HC // m):
                    rows = slice(2 * m * n, 2 * m * n + m)
                    act.activation(AT[rows, :, 2 * m * n + m:2 * m * n + 2 * m],
                                   lv(j).rearrange("p (c t) -> p c t", t=HC)[rows, :, m * n:m * n + m],
                                   ACT.Copy).then_inc(at_act, 1)

            def finish_a(h):
                copy_level(h, 7, 64)
                act.wait_ge(unit_done, 4 * h + 4)
                act.wait_ge(q_ready, h + 1)
                act.activation(SIG[:], PJ[1][:], ACT.Sigmoid).then_inc(gsig_ready, 1)

            def finish_b(h):
                act.wait_ge(kdtr_done, h + 1)
                act.activation(X1[:], R[:], ACT.Copy).then_inc(kd_ready, 1)
                act.wait_ge(o_done, h + 1)
                act.activation(X1[:], R[:], ACT.Square).then_inc(sq_ready, 1)

            def finish_c(h):
                act.wait_ge(mean_done, h + 1)
                act.activation(S[:], LV[:], ACT.Sqrt, bias=eps[:, 0:1]).then_inc(orms_ready, 1)

            def head(i, first=False, last=False):
                if not first:
                    finish_a(i - 1)
                split_hi(2 * i, 1)
                if not first:
                    finish_b(i - 1)
                act.wait_ge(unit_done, 4 * i + 1)
                if not first:
                    act.wait_ge(tree, TS * (i - 1) + 4)
                act.activation(F, PJ[0][:], ACT.Sigmoid).then_inc(fsig_ready, 1)
                split_hi(2 * i + 1, 0)
                if not first:
                    finish_c(i - 1)
                act.wait_ge(unit_done, 4 * i + 2)
                if not first:
                    act.wait_ge(gate_ready, i)
                act.activation(SIG[:], PJ[1][:], ACT.Sigmoid).then_inc(qsig_ready, 1)
                split_hi(2 * i + 1, 1)
                act.wait_ge(unit_done, 4 * i + 3)
                if not first:
                    act.wait_ge(mean_done, i)
                act.activation(X1[:], PJ[0][:], ACT.Copy).then_inc(vT_ready, 1)
                split_hi(2 * i + 2, 0)
                act.wait_ge(vtr_done, i + 1)
                act.activation(V[:], R[:], ACT.Copy).then_inc(v_ready, 1)
                copy_level(i, 6, 32)

            act.wait_ge(hhi_ready, TT)
            head(0, first=True)
            with act.Fori(1, HEADS) as i:
                head(i)

            def group(g, first=False):
                i = g + HEADS
                if first:
                    finish_a(HEADS - 1)
                else:
                    act.wait_ge(unit_done, 4 * i)
                    act.wait_ge(pgate_ready, 2 * g - 1)
                    act.activation(SIG[:], PJ[1][:], ACT.Sigmoid).then_inc(psig_ready, 1)
                split_hi(2 * i, 1)
                if first:
                    finish_b(HEADS - 1)
                act.wait_ge(unit_done, 4 * i + 1)
                if first:
                    act.wait_ge(kdtr_done, HEADS)
                act.activation(K, PJ[0][:], ACT.Copy).then_inc(u_ready, 1)
                split_hi(2 * i + 1, 0)
                if first:
                    finish_c(HEADS - 1)
                act.wait_ge(pw_loaded, 16 * g + 16)
                if not first:
                    act.wait_ge(mix_done, 2 * g)
                act.activation(m_hi[:, T:], X1[:, 0:2 * PT * P], ACT.Copy).then_inc(pwhi_ready, 1)
                act.wait_ge(pool_dd, 2 * g + 1)
                act.activation(m_hi[:, 0:T], Q, ACT.Copy).then_inc(dhi_ready, 1)
                act.wait_ge(unit_done, 4 * i + 2)
                if first:
                    act.wait_ge(gate_ready, HEADS)
                else:
                    act.wait_ge(pgate_ready, 2 * g)
                act.activation(SIG[:], PJ[1][:], ACT.Sigmoid).then_inc(psig_ready, 1)
                split_hi(2 * i + 1, 1)
                act.wait_ge(unit_done, 4 * i + 3)
                act.activation(F, PJ[0][:], ACT.Copy).then_inc(u_ready, 1)
                split_hi(2 * i + 2, 0)
                act.wait_ge(pool_dd, 2 * g + 2)
                act.wait_ge(mix_done, 2 * g + 1)
                act.activation(m_hi[:, 0:T], Q, ACT.Copy).then_inc(dhi_ready, 1)

            group(0, first=True)
            with act.Fori(1, GROUPS) as g:
                group(g)
            act.wait_ge(unit_done, UNITS)
            act.wait_ge(pgate_ready, 2 * GROUPS - 1)
            act.activation(SIG[:], PJ[1][:], ACT.Sigmoid).then_inc(psig_ready, 1)

            def y_hi(o, j, slot):
                act.wait_ge(consts, N_CONSTS)
                act.wait_ge(unit_done, UNITS + SLOTS * o + j - 1)
                act.activation(m_hi[:, slot * HALF:(slot + 1) * HALF].rearrange("p (a n) -> p a n", a=1),
                               Y[:, ds(j, 1), o * HALF:(o + 1) * HALF], ACT.Copy).then_inc(yhi_ready, 1)

            def out_pair(o, j):
                y_hi(o, 2 * j, 0)
                split_hi((UNITS + SLOTS * o) // 2 + j, 1)
                y_hi(o, 2 * j + 1, 1)
                split_hi((UNITS + SLOTS * o) // 2 + j + 1, 0)

            def tile_rms(n):
                act.wait_ge(res_ready, n + 1)
                if n:
                    act.wait_ge(fss_ready, n)
                act.activation(X1[:], RES[n % OT], ACT.Square, accum_out=ss[:, n:n + 1]).then_inc(fss_ready, 1)
                act.wait_ge(fss_ready, n + 1)
                act.activation(rms[:, n:n + 1], ss[:, n:n + 1], ACT.Sqrt, bias=eps[:, 0:1],
                               scale=1.0 / D).then_inc(frms_ready, 1)

            act.wait_ge(mix_done, 2 * GROUPS)
            for o in range(OG):
                if o == 0:
                    out_pair(0, 0)
                    act.wait_ge(py_ready, PT * GROUPS)
                else:
                    y_hi(o, 0, 0)
                    split_hi((UNITS + SLOTS * o) // 2, 1)
                    tile_rms(OT * (o - 1))
                    y_hi(o, 1, 1)
                    tile_rms(OT * (o - 1) + 1)
                    split_hi((UNITS + SLOTS * o) // 2 + 1, 0)
                    tile_rms(OT * (o - 1) + 2)
                    tile_rms(OT * (o - 1) + 3)
                with act.Fori(1, SLOTS // 2 - 1) as j:
                    out_pair(o, j)
                if o < OG - 1:
                    out_pair(o, SLOTS // 2 - 1)
            y_hi(OG - 1, SLOTS - 2, 0)
            split_hi((UNITS + SLOTS * OG) // 2 - 1, 1)
            y_hi(OG - 1, SLOTS - 1, 1)
            for t in range(OT):
                tile_rms(OT * (OG - 1) + t)

        @block.vector
        def _(dve):
            def split_lo(n, slot):
                dve.wait_ge(whi_ready, n + 1)
                dve.tensor_tensor(w_lo[:, slot, :], w_raw[:, slot, :], w_hi[:, slot, :].bitcast(f32),
                                  ALU.subtract).then_inc(wlo_ready, 1)

            dve.wait_ge(params_loaded, 48)
            dve.tensor_tensor(lbm[:], lbl[:, 0, :], lbl[:, 1, :], ALU.max).then_inc(lb_step, 1)
            dve.wait_ge(lb_step, 1)
            for r in range(2):
                dve.tensor_tensor(lbl[:, r, :], lbl[:, r, :], lbm[:], ALU.subtract).then_inc(lb_step, 1)
            dve.wait_ge(lb_exp, 1)
            dve.tensor_tensor(lbm[:], lbl[:, 0, :], lbl[:, 1, :], ALU.add).then_inc(lb_step, 1)
            dve.wait_ge(lb_step, 4)
            dve.reciprocal(omlb[:], lbm[:]).then_inc(lb_step, 1)
            dve.wait_ge(lb_step, 5)
            dve.tensor_tensor(lb[:], lbl[:, 0, :], omlb[:], ALU.mult).then_inc(lb_step, 1)
            dve.wait_ge(lb_step, 6)
            dve.tensor_scalar(omlb[:], lb[:], -1.0, 1.0, ALU.mult, ALU.add).then_inc(lb_step, 1)

            def low_h(t):
                dve.wait_ge(hhi_ready, t + 1)
                cols = slice(t * P, (t + 1) * P)
                dve.tensor_tensor(h_lo[:, :, cols], BANKS[t % 4][:].rearrange("p (k n) -> p k n", n=P),
                                  h_hi[:, :, cols].bitcast(f32), ALU.subtract).then_inc(hlo_ready, 1)

            dve.wait_ge(grow_loaded, 16)
            for t in range(TT):
                xt = Y[:, SLOTS - TT + t, :]
                dve.wait_ge(rms_ready, t + 1)
                dve.reciprocal(rin[:, t:t + 1], rms[:, t:t + 1]).then_inc(rin_ready, 1)
                dve.wait_ge(rin_ready, t + 1)
                dve.scalar_tensor_tensor(out=xt, in0=xt, scalar=rin[:, t:t + 1], in1=S[:],
                                         op0=ALU.mult, op1=ALU.mult).then_inc(xn_ready, 1)
                if t:
                    low_h(t - 1)
            split_lo(0, 0)
            low_h(TT - 1)

            def column(b, i):
                return b[:, ds(i, 1)]

            def tree_stage(h, k, m):
                for b, half in ((K, 0), (Q, 1)):
                    other = seg_total(m).rearrange("p (n two) -> p n two", two=2)[:, :, 1 - half:2 - half]
                    dve.tensor_tensor(halves(b, m, half), halves(b, m, half),
                                      other.to_broadcast([P, T // (2 * m), m]), ALU.mult).then_inc(tree, 1)
                tot = seg_total(m).rearrange("p (n two) -> p n two", two=2)
                dve.tensor_tensor(seg_total(2 * m), tot[:, :, 0], tot[:, :, 1], ALU.mult).then_inc(tree, 1)

            def masked_copy(h, j, k, m):
                which = 0 if j == 0 else 1
                dst = AT[:].rearrange("p c (n two m) -> p c n two m", two=2, m=m)[:, :, :, which, :]
                src = lv(j).rearrange("p (c n m) -> p c n m", c=TT, m=m)
                mask = masks[:, k:k + 1, :].bitcast(u32).rearrange("p a (n m) -> p a n m", m=m)
                dve.copy_predicated(dst, mask.to_broadcast([P, TT, HC // m, m]), src).then_inc(at_dve, 1)

            def finish_a(h):
                dve.wait_ge(lvl_done, LVLS * h + 8)
                dve.wait_ge(tree, TS * h + 19)
                tree_stage(h, 19, 64)

            def finish_b(h):
                dve.wait_ge(gsig_ready, h + 1)
                if not (isinstance(h, int) and h == 0):
                    dve.wait_ge(y_ready, h)
                dve.tensor_tensor(GATE[:], PJ[1][:], SIG[:], ALU.mult).then_inc(gate_ready, 1)
                dve.wait_ge(kv_done, h + 1)
                dve.tensor_copy(S[:, C:2 * C], R[:, 0:C]).then_inc(state, 1)
                for c in range(1, TT - 1):
                    dve.wait_ge(state, (TT - 1) * h + c)
                    o = GOFF[C] + c
                    dve.scalar_tensor_tensor(out=S[:, (c + 1) * C:(c + 2) * C], in0=S[:, c * C:(c + 1) * C],
                                             scalar=G[:, o:o + 1], in1=R[:, c * C:(c + 1) * C],
                                             op0=ALU.mult, op1=ALU.add).then_inc(state, 1)
                dve.wait_ge(sq_ready, h + 1)
                dve.wait_ge(gate_ready, h + 1)
                dve.scalar_tensor_tensor(out=GATE[:], in0=R[:], scalar=column(rg, h), in1=GATE[:],
                                         op0=ALU.mult, op1=ALU.mult).then_inc(oy_ready, 1)

            def finish_c(h):
                dve.wait_ge(orms_ready, h + 1)
                dve.reciprocal(S[:], S[:]).then_inc(orin_ready, 1)
                dve.wait_ge(orin_ready, h + 1)
                dve.tensor_tensor(Y[:, ds(h, 1), :].rearrange("p a t -> p (a t)"), GATE[:], S[:],
                                  ALU.mult).then_inc(y_ready, 1)

            def head(i, first=False):
                if not first:
                    finish_a(i - 1)
                split_lo(4 * i + 1, 1)
                if not first:
                    finish_b(i - 1)
                dve.wait_ge(fsig_ready, i + 1)
                dve.tensor_scalar(F, F, column(omlb, i), column(lb, i), ALU.mult, ALU.add).then_inc(fk_ready, 1)
                dve.wait_ge(fk_ready, 2 * i + 1)
                dve.tensor_scalar(K, F, -1.0, 1.0, ALU.mult, ALU.add).then_inc(fk_ready, 1)
                split_lo(4 * i + 2, 0)
                if not first:
                    finish_c(i - 1)
                dve.wait_ge(qsig_ready, i + 1)
                if not first:
                    dve.wait_ge(o_done, i)
                dve.tensor_tensor(Q, PJ[1][:], SIG[:], ALU.mult).then_inc(q_ready, 1)
                split_lo(4 * i + 3, 1)
                dve.wait_ge(fk_ready, 2 * i + 2)
                dve.wait_ge(lvl_done, LVLS * i + 1)
                dve.tensor_tensor(halves(K, 1, 0), halves(K, 1, 0), halves(F, 1, 1), ALU.mult).then_inc(tree, 1)
                masked_copy(i, 0, 0, 1)
                dve.wait_ge(at_dve, AD * i + 1)
                dve.wait_ge(lvl_done, LVLS * i + 2)
                dve.tensor_tensor(Q, Q, F, ALU.mult).then_inc(tree, 1)
                dve.wait_ge(tree, TS * i + 2)
                dve.tensor_tensor(halves(Q, 1, 1), halves(Q, 1, 1), halves(F, 1, 0), ALU.mult).then_inc(tree, 1)
                dve.tensor_tensor(seg_total(2), halves(F, 1, 0).rearrange("p n m -> p (n m)"),
                                  halves(F, 1, 1).rearrange("p n m -> p (n m)"), ALU.mult).then_inc(tree, 1)
                masked_copy(i, 1, 1, 1)
                for k, m in enumerate(LEVELS[:-1]):
                    dve.wait_ge(lvl_done, LVLS * i + 3 + k)
                    dve.wait_ge(tree, TS * i + 4 + 3 * k)
                    if k < 4:
                        dve.wait_ge(at_dve, AD * i + 2 + k)
                    tree_stage(i, 4 + 3 * k, m)
                    if k < 4:
                        masked_copy(i, 2 + k, 2 + k, m)
                    if k == 1:
                        split_lo(4 * i + 4, 0)

            dve.wait_ge(consts, N_CONSTS)
            head(0, first=True)
            with dve.Fori(1, HEADS) as i:
                head(i)

            steps = [0]

            def done(ins):
                ins.then_inc(pool_step, 1)
                steps[0] += 1

            def pooled(g, c, u):
                w = 2 << g
                dve.wait_ge(u_ready, 2 * g + c + 1)
                if g or c:
                    dve.wait_ge(dlo_ready, 2 * g + c)
                bufs = [Gp, Qp]
                src = u
                for k in range(g + 1):
                    dst = bufs[k % 2]
                    sh = 1 << k
                    done(dve.tensor_tensor(dst[:, PAD:], src[:, PAD:], src[:, PAD - sh:PAD + T - sh], ALU.add))
                    dve.wait_ge(pool_step, steps[0])
                    src = dst
                n = w - 1
                done(dve.tensor_tensor(fix[:, 0:n], src[:, PAD:PAD + n], rcount[:, 0:n], ALU.mult))
                dve.wait_ge(pool_step, steps[0])
                done(dve.scalar_tensor_tensor(out=Q, in0=src[:, PAD:], scalar=1.0 / w, in1=u[:, PAD:],
                                              op0=ALU.mult, op1=ALU.subtract))
                dve.wait_ge(pool_step, steps[0])
                dve.tensor_tensor(Q[:, 0:n], fix[:, 0:n], u[:, PAD:PAD + n], ALU.subtract).then_inc(pool_dd, 1)

            def low_dd(g, c):
                dve.wait_ge(dhi_ready, 2 * g + c + 1)
                dve.tensor_tensor(m_lo[:, 0:T], Q, m_hi[:, 0:T].bitcast(f32), ALU.subtract).then_inc(dlo_ready, 1)

            def pool_out(g):
                n = HEADS + PT * g
                dve.wait_ge(psig_ready, 2 * g + 2)
                dve.tensor_tensor(S[:], PJ[1][:], SIG[:], ALU.mult).then_inc(pgate_ready, 1)
                dve.wait_ge(mix_done, 2 * g + 2)
                dve.scalar_tensor_tensor(out=Y[:, n, :], in0=LV[:], scalar=psc[:, PT * g:PT * g + 1], in1=GATE[:],
                                         op0=ALU.mult, op1=ALU.mult).then_inc(py_ready, 1)
                dve.wait_ge(pgate_ready, 2 * g + 2)
                dve.scalar_tensor_tensor(out=Y[:, n + 1, :], in0=R[:], scalar=psc[:, PT * g + 1:PT * g + 2],
                                         in1=S[:], op0=ALU.mult, op1=ALU.mult).then_inc(py_ready, 1)

            for g in range(GROUPS):
                i = HEADS + g
                if g == 0:
                    finish_a(HEADS - 1)
                split_lo(4 * i + 1, 1)
                if g == 0:
                    finish_b(HEADS - 1)
                else:
                    pool_out(g - 1)
                split_lo(4 * i + 2, 0)
                if g == 0:
                    finish_c(HEADS - 1)
                pooled(g, 0, Kp)
                dve.wait_ge(pwhi_ready, g + 1)
                dve.tensor_tensor(m_lo[:, T:], X1[:, 0:2 * PT * P], m_hi[:, T:].bitcast(f32),
                                  ALU.subtract).then_inc(pwlo_ready, 1)
                low_dd(g, 0)
                dve.wait_ge(psig_ready, 2 * g + 1)
                if g == 0:
                    dve.wait_ge(y_ready, HEADS)
                else:
                    dve.wait_ge(py_ready, 2 * g)
                dve.tensor_tensor(GATE[:], PJ[1][:], SIG[:], ALU.mult).then_inc(pgate_ready, 1)
                split_lo(4 * i + 3, 1)
                pooled(g, 1, Fp)
                split_lo(4 * i + 4, 0)
                dve.wait_ge(mix_done, 2 * g + 1)
                low_dd(g, 1)
            pool_out(GROUPS - 1)

            def y_lo(o, j, slot):
                cols = slice(slot * HALF, (slot + 1) * HALF)
                dve.wait_ge(yhi_ready, SLOTS * o + j + 1)
                dve.tensor_tensor(m_lo[:, cols].rearrange("p (a n) -> p a n", a=1),
                                  Y[:, ds(j, 1), o * HALF:(o + 1) * HALF],
                                  m_hi[:, cols].bitcast(f32).rearrange("p (a n) -> p a n", a=1),
                                  ALU.subtract).then_inc(ylo_ready, 1)

            def out_pair(o, j):
                n = UNITS + SLOTS * o + 2 * j
                y_lo(o, 2 * j, 0)
                split_lo(n + 1, 1)
                y_lo(o, 2 * j + 1, 1)
                split_lo(n + 2, 0)

            def residual(n):
                t = n % OT
                if t < OT - 1:
                    dve.wait_ge(tile_done, (OT - 1) * (n // OT) + t + 1)
                else:
                    dve.wait_ge(unit_done, UNITS + SLOTS * (n // OT + 1))
                dve.wait_ge(xres_loaded[t], 16 * (n // OT) + 16)
                if n >= OT:
                    dve.wait_ge(out_stored[t], 16 * (n // OT))
                dve.tensor_tensor(RES[t], BANKS[t][:], (Q, K, F, G)[t], ALU.add).then_inc(res_ready, 1)

            def finish_tile(n):
                t = n % OT
                dve.wait_ge(frms_ready, n + 1)
                dve.reciprocal(rin[:, n:n + 1], rms[:, n:n + 1]).then_inc(frin_ready, 1)
                dve.wait_ge(frin_ready, n + 1)
                dve.wait_ge(gfin_loaded, 16)
                dve.scalar_tensor_tensor(out=RES[t], in0=RES[t], scalar=rin[:, n:n + 1], in1=V[:],
                                         op0=ALU.mult, op1=ALU.mult).then_inc(fin_ready, 1)

            for o in range(OG):
                if o == 0:
                    out_pair(0, 0)
                else:
                    n0, n = OT * (o - 1), UNITS + SLOTS * o
                    y_lo(o, 0, 0)
                    residual(n0)
                    residual(n0 + 1)
                    split_lo(n + 1, 1)
                    residual(n0 + 2)
                    y_lo(o, 1, 1)
                    residual(n0 + 3)
                    split_lo(n + 2, 0)
                    for t in range(OT):
                        finish_tile(n0 + t)
                with dve.Fori(1, SLOTS // 2 - 1) as j:
                    out_pair(o, j)
                if o < OG - 1:
                    out_pair(o, SLOTS // 2 - 1)
            y_lo(OG - 1, SLOTS - 2, 0)
            split_lo(UNITS + SLOTS * OG - 1, 1)
            y_lo(OG - 1, SLOTS - 1, 1)
            n0 = OT * (OG - 1)
            for t in range(OT):
                residual(n0 + t)
                if t:
                    finish_tile(n0 + t - 1)
            finish_tile(n0 + OT - 1)

        @block.tensor
        def _(pe):
            pe.wait_ge(consts, N_CONSTS)
            for t in range(TT):
                pe.wait_ge(xn_ready, t + 1)
                if t >= 4:
                    pe.wait_ge(hlo_ready, t - 3)
                for k in range(KT):
                    mm = pe.transpose(BANKS[t % 4][:, k * P:(k + 1) * P],
                                      Y[:, SLOTS - TT + t, k * P:(k + 1) * P], ident[:])
                mm.then_inc(xT_ready, 1)
            pe.wait_ge(hlo_ready, TT)

            def steps(slot, lo, hi):
                for k in range(lo, hi):
                    cols = slice(k * P, (k + 1) * P)
                    for a, b, first, last in ((w_hi, h_hi, True, False), (w_hi, h_lo, False, False),
                                              (w_lo, h_hi, False, True)):
                        for h in range(NH):
                            mm = pe.matmul(PJ[slot][:, h * HALF:(h + 1) * HALF], a[:, slot, cols],
                                           b[:, k, h * HALF:(h + 1) * HALF],
                                           start=(k == 0 and first), stop=(k == KT - 1 and last),
                                           skip_group_check=True)
                if hi == KT:
                    mm.then_inc(unit_done, 1)

            def chunk(b, c):
                return b[:, c * C:(c + 1) * C]

            def level(h, j):
                if j < 2:
                    if not (isinstance(h, int) and h == 0):
                        pe.wait_ge(orms_ready, h)
                else:
                    pe.wait_ge(at_dve, AD * h + j - 1)
                if j == 0:
                    pe.wait_ge(q_ready, h + 1)
                    m, which = 1, 0
                elif j == 1:
                    pe.wait_ge(tree, TS * h + 1)
                    m, which = 1, 1
                else:
                    pe.wait_ge(tree, TS * h + 4 + 3 * (j - 2))
                    m, which = LEVELS[j - 2], 1
                for c in range(TT):
                    mm = pe.matmul(lv(j)[:, c * HC:(c + 1) * HC], chunk(K, c), halves(chunk(Q, c), m, which),
                                   start=True, stop=True)
                mm.then_inc(lvl_done, 1)

            def v_transposes(h):
                pe.wait_ge(vT_ready, h + 1)
                if not (isinstance(h, int) and h == 0):
                    pe.wait_ge(oy_ready, h)
                for c in range(TT):
                    mm = pe.transpose(chunk(R, c), chunk(X1, c), ident[:])
                mm.then_inc(vtr_done, 1)

            def k_transposes(h):
                pe.wait_ge(tree, TS * h + TS)
                pe.wait_ge(v_ready, h + 1)
                for c in range(TT):
                    mm = pe.transpose(chunk(R, c), chunk(K, c), ident[:])
                mm.then_inc(kdtr_done, 1)

            def outer_products(h):
                pe.wait_ge(kd_ready, h + 1)
                for c in range(TT):
                    mm = pe.matmul(chunk(R, c), chunk(X1, c), chunk(V, c), start=True, stop=True)
                mm.then_inc(kv_done, 1)

            def readout(h):
                pe.wait_ge(at_dve, AD * h + AD)
                pe.wait_ge(at_act, AA * h + AA)
                pe.wait_ge(state, (TT - 1) * (h + 1))
                for c in range(TT):
                    mm = pe.matmul(chunk(R, c), chunk(V, c), AT[:, c, :], start=True, stop=(c == 0))
                    if c:
                        mm = pe.matmul(chunk(R, c), chunk(S, c), chunk(Q, c), start=False, stop=True)
                mm.then_inc(o_done, 1)

            def means(h):
                pe.wait_ge(sq_ready, h + 1)
                for k in range(NH):
                    mm = pe.matmul(LV[:, k * HALF:(k + 1) * HALF], mean_w[:], X1[:, k * HALF:(k + 1) * HALF],
                                   start=True, stop=True)
                mm.then_inc(mean_done, 1)

            def head(i, first=False):
                h_prev = i - 1
                pe.wait_ge(wlo_ready, 4 * i + 1)
                if not first:
                    pe.wait_ge(vT_ready, i)
                steps(0, 0, 2)
                if not first:
                    k_transposes(h_prev)
                steps(0, 2, 4)
                if not first:
                    outer_products(h_prev)
                steps(0, 4, 7)
                if not first:
                    readout(h_prev)
                steps(0, 7, 8)
                pe.wait_ge(wlo_ready, 4 * i + 2)
                if not first:
                    pe.wait_ge(gate_ready, i)
                steps(1, 0, 1)
                if not first:
                    means(h_prev)
                steps(1, 1, 8)
                pe.wait_ge(wlo_ready, 4 * i + 3)
                pe.wait_ge(fsig_ready, i + 1)
                steps(0, 0, 2)
                level(i, 0)
                steps(0, 2, 3)
                level(i, 1)
                steps(0, 3, 6)
                level(i, 2)
                steps(0, 6, 8)
                pe.wait_ge(wlo_ready, 4 * i + 4)
                pe.wait_ge(q_ready, i + 1)
                level(i, 3)
                steps(1, 0, 2)
                level(i, 4)
                steps(1, 2, 3)
                v_transposes(i)
                steps(1, 3, 4)
                level(i, 5)
                steps(1, 4, 6)
                level(i, 6)
                steps(1, 6, 8)
                level(i, 7)

            head(0, first=True)
            with pe.Fori(1, HEADS) as i:
                head(i)

            def mix(g, c):
                pe.wait_ge(dlo_ready, 2 * g + c + 1)
                if c == 0:
                    pe.wait_ge(pwlo_ready, g + 1)
                for d, dst in enumerate((LV, R)):
                    cols = slice(T + c * PT * P + d * P, T + c * PT * P + (d + 1) * P)
                    for h in range(NH):
                        tok = slice(h * HALF, (h + 1) * HALF)
                        for k, (a, b) in enumerate(((m_hi, m_hi), (m_hi, m_lo), (m_lo, m_hi))):
                            mm = pe.matmul(dst[:, tok], a[:, cols], b[:, tok], start=(c == 0 and k == 0),
                                           stop=(c == PT - 1 and k == 2), skip_group_check=True)
                mm.then_inc(mix_done, 1)

            def group(g, first=False):
                i = g + HEADS
                pe.wait_ge(wlo_ready, 4 * i + 1)
                if first:
                    pe.wait_ge(vT_ready, HEADS)
                else:
                    pe.wait_ge(u_ready, 2 * g)
                steps(0, 0, 2)
                if first:
                    k_transposes(HEADS - 1)
                steps(0, 2, 4)
                if first:
                    outer_products(HEADS - 1)
                steps(0, 4, 7)
                if first:
                    readout(HEADS - 1)
                steps(0, 7, 8)
                pe.wait_ge(wlo_ready, 4 * i + 2)
                if first:
                    pe.wait_ge(gate_ready, HEADS)
                else:
                    pe.wait_ge(pgate_ready, 2 * g)
                steps(1, 0, 1)
                if first:
                    means(HEADS - 1)
                steps(1, 1, 8)
                pe.wait_ge(wlo_ready, 4 * i + 3)
                pe.wait_ge(u_ready, 2 * g + 1)
                steps(0, 0, 4)
                if first:
                    pe.wait_ge(y_ready, HEADS)
                else:
                    pe.wait_ge(py_ready, 2 * g)
                mix(g, 0)
                steps(0, 4, 8)
                pe.wait_ge(wlo_ready, 4 * i + 4)
                pe.wait_ge(pgate_ready, 2 * g + 1)
                steps(1, 0, 8)
                mix(g, 1)

            group(0, first=True)
            with pe.Fori(1, GROUPS) as g:
                group(g)

            def out_unit(o, n, slot, first=False, last=False):
                pe.wait_ge(wlo_ready, n + 1)
                pe.wait_ge(ylo_ready, n - UNITS + 1)
                for t in range(OT):
                    if first:
                        if o:
                            pe.wait_ge(res_ready, OT * (o - 1) + t + 1)
                        elif t == 0:
                            pe.wait_ge(u_ready, 2 * GROUPS)
                        elif t == 1:
                            pe.wait_ge(pgate_ready, 2 * GROUPS)
                        else:
                            pe.wait_ge(py_ready, 2 * GROUPS - 3 + t)
                    tok = slice(slot * HALF + t * P, slot * HALF + (t + 1) * P)
                    for k, (a, b) in enumerate(((m_hi, w_hi), (m_hi, w_lo), (m_lo, w_hi))):
                        for h in range(D // HALF):
                            cols = slice(h * HALF, (h + 1) * HALF)
                            mm = pe.matmul(BANKS[t][:, cols], a[:, tok], b[:, slot, cols],
                                           start=(first and k == 0), stop=(last and k == 2),
                                           skip_group_check=True)
                    if last and t < OT - 1:
                        mm.then_inc(tile_done, 1)
                mm.then_inc(unit_done, 1)

            for o in range(OG):
                n0 = UNITS + SLOTS * o
                out_unit(o, n0, 0, first=True)
                out_unit(o, n0 + 1, 1)
                with pe.Fori(1, SLOTS // 2 - 1) as j:
                    out_unit(o, n0 + 2 * j, 0)
                    out_unit(o, n0 + 2 * j + 1, 1)
                out_unit(o, n0 + SLOTS - 2, 0)
                out_unit(o, n0 + SLOTS - 1, 1, last=True)


_INS = ['x', 'norm1_g', 'w_in', 'pool_w', 'pool_scale', 'lb_logits', 'rec_norm_g', 'w_out', 'final_norm_g']


def kernel(**inputs):
    import numpy as _np
    import concourse.bacc as _bacc
    from concourse import mybir as _mybir
    from concourse.bass_utils import run_bass_kernel_spmd as _run

    nc = _bacc.Bacc("TRN2", target_bir_lowering=False, num_devices=1)
    arrays, args = {}, []
    for name in _INS:
        a = _np.ascontiguousarray(inputs[name])
        arrays[f"in_{name}_dram"] = a
        args.append(nc.dram_tensor(f"in_{name}_dram", a.shape, _mybir.dt.from_np(a.dtype), kind="ExternalInput").ap())
    shape = inputs["x"].shape
    args.append(nc.dram_tensor("out_0_dram", shape, _mybir.dt.float32, kind="ExternalOutput").ap())
    hybrid_pool_hgrn2_kernel(nc, *args)
    r = _run(nc, [arrays], core_ids=[0])
    return r.results[0]["out_0_dram"]
```

```python
import concourse.bass as bass
from concourse import mybir
from contextlib import ExitStack


def hybrid_pool_hgrn2_kernel(nc, x, norm1_g, w_in, pool_w, pool_scale, lb_logits,
                             rec_norm_g, w_out, final_norm_g, out):
    f32 = mybir.dt.float32
    f32r = mybir.dt.float32r
    u32 = mybir.dt.uint32
    ALU = mybir.AluOpType
    ACT = mybir.ActivationFunctionType
    AX = mybir.AxisListType
    ds = bass.ds

    P = 128
    T, D = x.shape[1], x.shape[2]
    KT = D // P
    TT = T // P
    HALF = 512
    NH = T // HALF
    C = P
    HC = C // 2
    B = 32
    HEADS = D // P
    GROUPS = pool_w.shape[1]
    PT = D // GROUPS // P
    EPS = 1e-6
    PAD = 16
    BLOCKS = HEADS + GROUPS
    UNITS = 4 * BLOCKS
    SLOTS = HEADS + PT * GROUPS
    OG = 2
    OT = TT // OG

    POOL_IN, POOL_GATE, QC, FC, VC, GC = (k * D for k in range(6))

    w_in_v = w_in[0].rearrange("(k p) n -> p k n", p=P)
    w_out_v = w_out[0].rearrange("(s p) n -> p s n", p=P)
    pool_w_v = pool_w[0].rearrange("g (c p) n -> g p c n", p=P)
    x_v = x[0].rearrange("(t p) d -> t p d", p=P)
    out_v = out[0].rearrange("(t p) d -> t p d", p=P)

    ctx = ExitStack()
    with ctx:
        def sb(name, shape, dt=f32):
            return ctx.enter_context(nc.sbuf_tensor(name, shape, dt))

        def sem(name):
            return ctx.enter_context(nc.semaphore(name))

        h_hi = sb("h_hi", [P, KT, T], f32r)
        h_lo = sb("h_lo", [P, KT, T], f32r)
        Y = sb("Y", [P, SLOTS, T])
        w_raw = sb("w_raw", [P, 2, KT * P])
        w_hi = sb("w_hi", [P, 2, KT * P], f32r)
        w_lo = sb("w_lo", [P, 2, KT * P], f32r)
        m_hi = sb("m_hi", [P, T + 2 * PT * P], f32r)
        m_lo = sb("m_lo", [P, T + 2 * PT * P], f32r)
        Qp = sb("Qp", [P, PAD + T])
        Kp = sb("Kp", [P, PAD + T])
        Fp = sb("Fp", [P, PAD + T])
        Gp = sb("Gp", [P, PAD + T])
        Q, K, F, G = (b[:, PAD:PAD + T] for b in (Qp, Kp, Fp, Gp))
        V = sb("V", [P, T])
        X1 = sb("X1", [P, T])
        AT = sb("AT", [P, TT, C])
        S = sb("S", [P, T])
        GATE = sb("GATE", [P, T])
        SIG = sb("SIG", [P, T])

        ident = sb("ident", [P, P])
        mean_w = sb("mean_w", [P, P], f32r)
        masks = sb("masks", [P, 6, HC])
        rcount = sb("rcount", [P, PAD])
        fix = sb("fix", [P, PAD])
        eps = sb("eps", [P, 1])
        lbl = sb("lbl", [P, 2, HEADS])
        lbm = sb("lbm", [P, HEADS])
        lb = sb("lb", [P, HEADS])
        omlb = sb("omlb", [P, HEADS])
        rg = sb("rg", [P, HEADS])
        psc = sb("psc", [P, HEADS])
        ss = sb("ss", [P, TT])
        rms = sb("rms", [P, TT])
        rin = sb("rin", [P, TT])

        PJ = [ctx.enter_context(nc.psum_tensor(f"PJ{i}", [P, T], f32)) for i in range(2)]
        LV = ctx.enter_context(nc.psum_tensor("LV", [P, T], f32))
        R = ctx.enter_context(nc.psum_tensor("R", [P, T], f32))
        BANKS = [PJ[0], LV, PJ[1], R]
        XT = [LV, R]

        x_loaded = [sem(f"x_loaded{t}") for t in range(TT)]
        params_loaded = sem("params_loaded")
        grow_loaded = sem("grow_loaded")
        w_loaded = [sem(f"w_loaded{i}") for i in range(2)]
        pw_loaded = sem("pw_loaded")
        xres_loaded = [sem(f"xres_loaded{t}") for t in range(OT)]
        gfin_loaded = sem("gfin_loaded")
        early_stored = [sem(f"early_stored{t}") for t in range(OT)]
        out_stored = [sem(f"out_stored{t}") for t in range(OT)]
        eps_ready = sem("eps_ready")
        ident_ready = sem("ident_ready")
        consts = sem("consts")
        const_step = sem("const_step")
        ss_ready = sem("ss_ready")
        rms_ready = sem("rms_ready")
        rin_ready = sem("rin_ready")
        xn_ready = sem("xn_ready")
        xT_ready = sem("xT_ready")
        hhi_ready = sem("hhi_ready")
        hlo_ready = sem("hlo_ready")
        lb_step = sem("lb_step")
        lb_exp = sem("lb_exp")
        whi_ready = sem("whi_ready")
        wlo_ready = sem("wlo_ready")
        unit_done = sem("unit_done")
        fsig_ready = sem("fsig_ready")
        qsig_ready = sem("qsig_ready")
        gsig_ready = sem("gsig_ready")
        vT_ready = sem("vT_ready")
        v_ready = sem("v_ready")
        kd_ready = sem("kd_ready")
        sq_ready = sem("sq_ready")
        sqhi_ready = sem("sqhi_ready")
        sqlo_ready = sem("sqlo_ready")
        orms_ready = sem("orms_ready")
        at_act = sem("at_act")
        at_dve = sem("at_dve")
        fk_ready = sem("fk_ready")
        q_ready = sem("q_ready")
        tree = sem("tree")
        state = sem("state")
        gate_ready = sem("gate_ready")
        oy_ready = sem("oy_ready")
        orin_ready = sem("orin_ready")
        y_ready = sem("y_ready")
        lvl_done = sem("lvl_done")
        vtr_done = sem("vtr_done")
        kdtr_done = sem("kdtr_done")
        kv_done = sem("kv_done")
        o_done = sem("o_done")
        mean_done = sem("mean_done")
        u_ready = sem("u_ready")
        pool_step = sem("pool_step")
        pool_dd = sem("pool_dd")
        dhi_ready = sem("dhi_ready")
        dlo_ready = sem("dlo_ready")
        pwhi_ready = sem("pwhi_ready")
        pwlo_ready = sem("pwlo_ready")
        psig_ready = sem("psig_ready")
        pgate_ready = sem("pgate_ready")
        mix_done = sem("mix_done")
        py_ready = sem("py_ready")
        yhi_ready = sem("yhi_ready")
        ylo_ready = sem("ylo_ready")
        tile_done = sem("tile_done")
        res_ready = sem("res_ready")
        fss_ready = sem("fss_ready")
        frms_ready = sem("frms_ready")
        frin_ready = sem("frin_ready")
        fin_ready = sem("fin_ready")

        LEVELS = [2, 4, 8, 16, 32, 64]
        LVLS = 2 + len(LEVELS)
        TS = 4 + 3 * len(LEVELS)
        AD, AA = 6, 3
        GOFF = {2: 0}
        for m in LEVELS:
            GOFF[2 * m] = GOFF[m] + T // m

        def seg_total(m):
            return F if m == 1 else G[:, GOFF[m]:GOFF[m] + T // m]

        def pair_half(b, m, which):
            return b.rearrange("p (n two m) -> p n two m", two=2, m=m)[:, :, which, :]

        def lv(j):
            return LV[:, (j % 2) * HALF:(j % 2 + 1) * HALF]

        block = ctx.enter_context(nc.Block())

        N_CONSTS = 5 + 2 + 4 + PAD
        RES = [AT[:].rearrange("p c t -> p (c t)"), GATE[:], S[:], SIG[:]]

        @block.gpsimd
        def _(pool):
            pool.memset(eps[:], EPS).then_inc(eps_ready, 1)
            pool.memset(ident[:], 0.0).then_inc(const_step, 1)
            pool.wait_ge(const_step, 1)
            pool.affine_select(out=ident[:], in_=ident[:], compare_op=ALU.not_equal, fill=1.0, base=0,
                               pattern=[[-1, P]], channel_multiplier=1).then_inc(ident_ready, 1)
            pool.memset(masks[:], 1.0).then_inc(const_step, 1)
            pool.wait_ge(const_step, 2)
            pool.affine_select(out=masks[:, 0, :], in_=masks[:, 0, :], compare_op=ALU.is_equal, fill=0.0,
                               base=0, pattern=[[-2, HC]], channel_multiplier=1).then_inc(const_step, 1)
            spans = [(1, 2, 2)] + [(1 + k, 2 * m, m) for k, m in enumerate(LEVELS[:4], 1)]
            for k, pair, width in spans:
                m = pair // 2
                mk = masks[:, k, :].rearrange("p (n m) -> p n m", m=m)
                pool.affine_select(out=mk, in_=mk, compare_op=ALU.is_ge, fill=0.0, base=0,
                                   pattern=[[-pair, HC // m], [0, m]], channel_multiplier=1).then_inc(const_step, 1)
            pool.wait_ge(const_step, 3 + len(spans))
            for k, pair, width in spans:
                m = pair // 2
                mk = masks[:, k, :].rearrange("p (n m) -> p n m", m=m)
                pool.affine_select(out=mk, in_=mk, compare_op=ALU.is_ge, fill=0.0, base=width - 1,
                                   pattern=[[pair, HC // m], [0, m]], channel_multiplier=-1).then_inc(consts, 1)
            pool.memset(mean_w[:].bitcast(f32), 1.0 / P).then_inc(consts, 1)
            pool.memset(AT[:], 0.0).then_inc(consts, 1)
            for b in (Qp, Kp, Fp, Gp):
                pool.memset(b[:, 0:PAD], 0.0).then_inc(consts, 1)
            for t in range(PAD):
                pool.memset(rcount[:, t:t + 1], 1.0 / (t + 1)).then_inc(consts, 1)
            for n in range(TT - OT):
                pool.wait_ge(fin_ready, n + 1)
                pool.dma_start(out_v[n], RES[n % OT]).then_inc(early_stored[n % OT], 16)
            for t in range(OT):
                pool.wait_ge(early_stored[t], 16 * (OG - 1))


        @block.sync
        def _(sp):
            def load_unit(n, slot, src, first=False):
                if not first:
                    sp.wait_ge(wlo_ready, n - 1)
                sp.dma_start(w_raw[:, slot, :].rearrange("p (k n) -> p k n", n=P), src).then_inc(w_loaded[slot], 16)

            def load_head_unit(i, u, first=False):
                load_unit(4 * i + u, u % 2, w_in_v[:, :, ds((FC, QC, VC, GC)[u] + i * P, P)], first)

            def load_group(g):
                for u, (base, c) in enumerate(((POOL_IN, 0), (POOL_IN, 1), (POOL_GATE, 0), (POOL_GATE, 1))):
                    load_unit(4 * (HEADS + g) + u, u % 2, w_in_v[:, :, ds(base + c * P + g * (PT * P), P)])

            def load_pool_w(g):
                if isinstance(g, int) and g == 0:
                    sp.wait_ge(mean_done, HEADS)
                else:
                    sp.wait_ge(pwlo_ready, g)
                sp.dma_start(X1[:, 0:2 * PT * P].rearrange("p (a c n) -> p a c n", a=1, c=PT),
                             pool_w_v[ds(g, 1)].rearrange("a p c n -> p a c n")).then_inc(pw_loaded, 16)

            def load_out_pair(n, row):
                for u in range(2):
                    sp.wait_ge(wlo_ready, n + u - 1)
                    sp.dma_start(w_raw[:, u, :].rearrange("p (a n) -> p a n", a=1),
                                 w_out_v[:, ds(row + u, 1), :]).then_inc(w_loaded[u], 16)

            for t in range(TT):
                sp.dma_start(Y[:, SLOTS - TT + t, :], x_v[t]).then_inc(x_loaded[t], 16)
                if t == 2 or t == 4:
                    load_head_unit(0, t // 2 - 1, first=True)
            for u in range(2, 4):
                load_head_unit(0, u)
            with sp.Fori(1, HEADS) as i:
                for u in range(4):
                    load_head_unit(i, u)
            load_group(0)
            load_pool_w(0)
            with sp.Fori(1, GROUPS) as g:
                load_group(g)
                load_pool_w(g)
            for o in range(OG):
                n0 = UNITS + SLOTS * o
                with sp.Fori(0, HEADS // 2) as j:
                    load_out_pair(n0 + 2 * j, (SLOTS - HEADS) + 2 * j)
                if o == 0:
                    sp.wait_ge(py_ready, PT * GROUPS)
                    sp.dma_start(V[:], final_norm_g.partition_broadcast(P)).then_inc(gfin_loaded, 16)
                for t, b in enumerate((Q, K, F, G)):
                    if o:
                        sp.wait_ge(res_ready, OT * (o - 1) + t + 1)
                    sp.dma_start(b, x_v[OT * o + t]).then_inc(xres_loaded[t], 16)
                with sp.Fori(0, (SLOTS - HEADS) // 2) as j:
                    load_out_pair(n0 + HEADS + 2 * j, 2 * j)

            for t in range(OT):
                sp.wait_ge(fin_ready, TT - OT + t + 1)
                sp.dma_start(out_v[TT - OT + t], RES[t]).then_inc(out_stored[t], 16)
            for t in range(OT):
                sp.wait_ge(out_stored[t], 16)

        @block.scalar
        def _(act):
            def split_hi(half_n, slot):
                act.wait_ge(w_loaded[slot], half_n * 16 + 16)
                if not (isinstance(half_n, int) and half_n == 0):
                    act.wait_ge(unit_done, half_n * 2 + slot - 1)
                act.activation(w_hi[:, slot, :], w_raw[:, slot, :], ACT.Copy).then_inc(whi_ready, 1)

            act.dma_start(S[:], norm1_g.partition_broadcast(P)).then_inc(grow_loaded, 16)
            with nc.allow_non_contiguous_dma("parameters of 4 KB, transposed by the load"):
                act.dma_start(lbl[:], lb_logits.rearrange("l (h p) -> p l h", p=P)).then_inc(params_loaded, 16)
                act.dma_start(rg[:], rec_norm_g[0].rearrange("(h p) -> p h", p=P)).then_inc(params_loaded, 16)
                act.dma_start(psc[:], pool_scale[0].rearrange("(h p) -> p h", p=P)).then_inc(params_loaded, 16)

            def token_rms(t):
                act.wait_ge(x_loaded[t], 16)
                if t:
                    act.wait_ge(ss_ready, t)
                act.activation(X1[:], Y[:, SLOTS - TT + t, :], ACT.Square,
                               accum_out=ss[:, t:t + 1]).then_inc(ss_ready, 1)
                act.wait_ge(ss_ready, t + 1)
                act.activation(rms[:, t:t + 1], ss[:, t:t + 1], ACT.Sqrt, bias=eps[:, 0:1],
                               scale=1.0 / D).then_inc(rms_ready, 1)

            def high_h(t):
                act.wait_ge(xT_ready, t + 1)
                act.activation(h_hi[:, :, t * P:(t + 1) * P], XT[t % 2][:].rearrange("p (k n) -> p k n", n=P),
                               ACT.Copy).then_inc(hhi_ready, 1)

            act.wait_ge(eps_ready, 1)
            act.activation(rms[:, 0:1], eps[:, 0:1], ACT.Sqrt).then_inc(rms_ready, 1)
            act.wait_ge(rms_ready, 1)
            token_rms(0)
            token_rms(1)
            for t in range(TT):
                if t + 2 < TT:
                    token_rms(t + 2)
                high_h(t)
                if t == 2:
                    split_hi(0, 0)
                if t == 4:
                    split_hi(0, 1)

            act.wait_ge(lb_step, 3)
            act.activation(lbl[:], lbl[:], ACT.Exp).then_inc(lb_exp, 1)

            def copy_level(h, j, m):
                act.wait_ge(lvl_done, LVLS * h + j + 1)
                act.wait_ge(at_dve, AD * h + AD)
                for n in range(HC // m):
                    rows = slice(2 * m * n, 2 * m * n + m)
                    act.activation(AT[rows, :, 2 * m * n + m:2 * m * n + 2 * m],
                                   lv(j).rearrange("p (c t) -> p c t", t=HC)[rows, :, m * n:m * n + m],
                                   ACT.Copy).then_inc(at_act, 1)

            def finish_a(h):
                copy_level(h, 7, 64)
                act.wait_ge(unit_done, 4 * h + 4)
                act.wait_ge(q_ready, h + 1)
                act.activation(SIG[:], PJ[1][:], ACT.Sigmoid).then_inc(gsig_ready, 1)

            def finish_b(h):
                act.wait_ge(kdtr_done, h + 1)
                act.activation(X1[:], R[:], ACT.Copy).then_inc(kd_ready, 1)
                act.wait_ge(o_done, h + 1)
                act.activation(X1[:], R[:], ACT.Square).then_inc(sq_ready, 1)
                act.wait_ge(sq_ready, h + 1)
                act.activation(m_hi[:, 0:T], X1[:], ACT.Copy).then_inc(sqhi_ready, 1)

            def finish_c(h):
                act.wait_ge(mean_done, h + 1)
                act.activation(S[:], LV[:], ACT.Sqrt, bias=eps[:, 0:1]).then_inc(orms_ready, 1)

            def head(i, first=False, last=False):
                if not first:
                    finish_a(i - 1)
                    split_hi(2 * i, 1)
                    finish_b(i - 1)
                act.wait_ge(unit_done, 4 * i + 1)
                if not first:
                    act.wait_ge(tree, TS * (i - 1) + 4)
                act.activation(F, PJ[0][:], ACT.Sigmoid).then_inc(fsig_ready, 1)
                split_hi(2 * i + 1, 0)
                if not first:
                    finish_c(i - 1)
                act.wait_ge(unit_done, 4 * i + 2)
                if not first:
                    act.wait_ge(gate_ready, i)
                act.activation(SIG[:], PJ[1][:], ACT.Sigmoid).then_inc(qsig_ready, 1)
                split_hi(2 * i + 1, 1)
                act.wait_ge(unit_done, 4 * i + 3)
                if not first:
                    act.wait_ge(sqlo_ready, i)
                act.activation(X1[:], PJ[0][:], ACT.Copy).then_inc(vT_ready, 1)
                split_hi(2 * i + 2, 0)
                act.wait_ge(vtr_done, i + 1)
                act.activation(V[:], R[:], ACT.Copy).then_inc(v_ready, 1)
                copy_level(i, 6, 32)

            act.wait_ge(consts, N_CONSTS)
            head(0, first=True)
            with act.Fori(1, HEADS) as i:
                head(i)

            def second_gate(g):
                act.wait_ge(unit_done, 4 * (HEADS + g) + 4)
                act.wait_ge(pgate_ready, 2 * g + 1)
                act.activation(SIG[:], PJ[1][:], ACT.Sigmoid).then_inc(psig_ready, 1)

            def group(g, first=False):
                i = g + HEADS
                if first:
                    finish_a(HEADS - 1)
                else:
                    second_gate(g - 1)
                split_hi(2 * i, 1)
                if first:
                    finish_b(HEADS - 1)
                act.wait_ge(unit_done, 4 * i + 1)
                act.activation(K, PJ[0][:], ACT.Copy).then_inc(u_ready, 1)
                split_hi(2 * i + 1, 0)
                if first:
                    finish_c(HEADS - 1)
                act.wait_ge(pw_loaded, 16 * g + 16)
                if not first:
                    act.wait_ge(mix_done, 2 * g)
                act.activation(m_hi[:, T:], X1[:, 0:2 * PT * P], ACT.Copy).then_inc(pwhi_ready, 1)
                act.wait_ge(pool_dd, 2 * g + 1)
                act.activation(m_hi[:, 0:T], Q, ACT.Copy).then_inc(dhi_ready, 1)
                act.wait_ge(unit_done, 4 * i + 2)
                act.activation(F, PJ[1][:], ACT.Copy).then_inc(u_ready, 1)
                split_hi(2 * i + 1, 1)
                act.wait_ge(mix_done, 2 * g + 1)
                act.wait_ge(pool_dd, 2 * g + 2)
                act.activation(m_hi[:, 0:T], Q, ACT.Copy).then_inc(dhi_ready, 1)
                act.wait_ge(unit_done, 4 * i + 3)
                if first:
                    act.wait_ge(gate_ready, HEADS)
                else:
                    act.wait_ge(pgate_ready, 2 * g)
                act.activation(SIG[:], PJ[0][:], ACT.Sigmoid).then_inc(psig_ready, 1)
                split_hi(2 * i + 2, 0)

            group(0, first=True)
            with act.Fori(1, GROUPS) as g:
                group(g)

            def y_hi(o, j, slot):
                act.wait_ge(consts, N_CONSTS)
                act.wait_ge(unit_done, UNITS + SLOTS * o + j - 1)
                act.activation(m_hi[:, slot * HALF:(slot + 1) * HALF].rearrange("p (a n) -> p a n", a=1),
                               Y[:, ds(j, 1), o * HALF:(o + 1) * HALF], ACT.Copy).then_inc(yhi_ready, 1)

            def out_pair(o, j):
                y_hi(o, 2 * j, 0)
                split_hi((UNITS + SLOTS * o) // 2 + j, 1)
                y_hi(o, 2 * j + 1, 1)
                split_hi((UNITS + SLOTS * o) // 2 + j + 1, 0)

            def tile_rms(n):
                act.wait_ge(res_ready, n + 1)
                if n:
                    act.wait_ge(fss_ready, n)
                act.activation(X1[:], RES[n % OT], ACT.Square, accum_out=ss[:, n:n + 1]).then_inc(fss_ready, 1)
                act.wait_ge(fss_ready, n + 1)
                act.activation(rms[:, n:n + 1], ss[:, n:n + 1], ACT.Sqrt, bias=eps[:, 0:1],
                               scale=1.0 / D).then_inc(frms_ready, 1)

            act.wait_ge(mix_done, 2 * GROUPS)
            for o in range(OG):
                if o == 0:
                    y_hi(0, 0, 0)
                    second_gate(GROUPS - 1)
                    split_hi(UNITS // 2, 1)
                    y_hi(0, 1, 1)
                    split_hi(UNITS // 2 + 1, 0)
                    act.wait_ge(py_ready, PT * GROUPS)
                else:
                    y_hi(o, 0, 0)
                    split_hi((UNITS + SLOTS * o) // 2, 1)
                    y_hi(o, 1, 1)
                    tile_rms(OT * (o - 1))
                    tile_rms(OT * (o - 1) + 1)
                    split_hi((UNITS + SLOTS * o) // 2 + 1, 0)
                    tile_rms(OT * (o - 1) + 2)
                    tile_rms(OT * (o - 1) + 3)
                with act.Fori(1, SLOTS // 2 - 1) as j:
                    out_pair(o, j)
                if o < OG - 1:
                    out_pair(o, SLOTS // 2 - 1)
            y_hi(OG - 1, SLOTS - 2, 0)
            split_hi((UNITS + SLOTS * OG) // 2 - 1, 1)
            y_hi(OG - 1, SLOTS - 1, 1)
            for t in range(OT):
                tile_rms(OT * (OG - 1) + t)

        @block.vector
        def _(dve):
            def split_lo(n, slot):
                dve.wait_ge(whi_ready, n + 1)
                dve.tensor_tensor(w_lo[:, slot, :], w_raw[:, slot, :], w_hi[:, slot, :].bitcast(f32),
                                  ALU.subtract).then_inc(wlo_ready, 1)

            def normalise(t):
                xt = Y[:, SLOTS - TT + t, :]
                dve.wait_ge(rms_ready, t + 2)
                dve.reciprocal(rin[:, t:t + 1], rms[:, t:t + 1]).then_inc(rin_ready, 1)
                dve.wait_ge(rin_ready, t + 1)
                dve.scalar_tensor_tensor(out=xt, in0=xt, scalar=rin[:, t:t + 1], in1=S[:],
                                         op0=ALU.mult, op1=ALU.mult).then_inc(xn_ready, 1)

            def low_h(t):
                dve.wait_ge(hhi_ready, t + 1)
                cols = slice(t * P, (t + 1) * P)
                dve.tensor_tensor(h_lo[:, :, cols], XT[t % 2][:].rearrange("p (k n) -> p k n", n=P),
                                  h_hi[:, :, cols].bitcast(f32), ALU.subtract).then_inc(hlo_ready, 1)

            dve.wait_ge(grow_loaded, 16)
            normalise(0)
            for t in range(TT):
                if t + 1 < TT:
                    normalise(t + 1)
                low_h(t)
                if t == 2:
                    split_lo(0, 0)
                if t == 4:
                    split_lo(1, 1)

            dve.wait_ge(params_loaded, 48)
            dve.tensor_tensor(lbm[:], lbl[:, 0, :], lbl[:, 1, :], ALU.max).then_inc(lb_step, 1)
            dve.wait_ge(lb_step, 1)
            for r in range(2):
                dve.tensor_tensor(lbl[:, r, :], lbl[:, r, :], lbm[:], ALU.subtract).then_inc(lb_step, 1)

            dve.wait_ge(lb_exp, 1)
            dve.tensor_tensor(lbm[:], lbl[:, 0, :], lbl[:, 1, :], ALU.add).then_inc(lb_step, 1)
            dve.wait_ge(lb_step, 4)
            dve.reciprocal(omlb[:], lbm[:]).then_inc(lb_step, 1)
            dve.wait_ge(lb_step, 5)
            dve.tensor_tensor(lb[:], lbl[:, 0, :], omlb[:], ALU.mult).then_inc(lb_step, 1)
            dve.wait_ge(lb_step, 6)
            dve.tensor_scalar(omlb[:], lb[:], -1.0, 1.0, ALU.mult, ALU.add).then_inc(lb_step, 1)
            dve.wait_ge(lb_step, 7)

            def column(b, i):
                return b[:, ds(i, 1)]

            def tree_stage(h, k, m):
                for b, half in ((K, 0), (Q, 1)):
                    other = seg_total(m).rearrange("p (n two) -> p n two", two=2)[:, :, 1 - half:2 - half]
                    dve.tensor_tensor(pair_half(b, m, half), pair_half(b, m, half),
                                      other.to_broadcast([P, T // (2 * m), m]), ALU.mult).then_inc(tree, 1)
                tot = seg_total(m).rearrange("p (n two) -> p n two", two=2)
                dve.tensor_tensor(seg_total(2 * m), tot[:, :, 0], tot[:, :, 1], ALU.mult).then_inc(tree, 1)

            def masked_copy(h, j, k, m):
                which = 0 if j == 0 else 1
                dst = AT[:].rearrange("p c (n two m) -> p c n two m", two=2, m=m)[:, :, :, which, :]
                src = lv(j).rearrange("p (c n m) -> p c n m", c=TT, m=m)
                mask = masks[:, k:k + 1, :].bitcast(u32).rearrange("p a (n m) -> p a n m", m=m)
                dve.copy_predicated(dst, mask.to_broadcast([P, TT, HC // m, m]), src).then_inc(at_dve, 1)

            def finish_a(h):
                dve.wait_ge(lvl_done, LVLS * h + 8)
                dve.wait_ge(tree, TS * h + 19)
                tree_stage(h, 19, 64)

            def finish_b(h):
                dve.wait_ge(gsig_ready, h + 1)
                if not (isinstance(h, int) and h == 0):
                    dve.wait_ge(y_ready, h)
                dve.tensor_tensor(GATE[:], PJ[1][:], SIG[:], ALU.mult).then_inc(gate_ready, 1)
                dve.wait_ge(kv_done, h + 1)
                dve.tensor_copy(S[:, C:2 * C], R[:, 0:C]).then_inc(state, 1)
                for c in range(1, TT - 1):
                    dve.wait_ge(state, (TT - 1) * h + c)
                    o = GOFF[C] + c
                    dve.scalar_tensor_tensor(out=S[:, (c + 1) * C:(c + 2) * C], in0=S[:, c * C:(c + 1) * C],
                                             scalar=G[:, o:o + 1], in1=R[:, c * C:(c + 1) * C],
                                             op0=ALU.mult, op1=ALU.add).then_inc(state, 1)
                dve.wait_ge(sq_ready, h + 1)
                dve.wait_ge(gate_ready, h + 1)
                dve.scalar_tensor_tensor(out=GATE[:], in0=R[:], scalar=column(rg, h), in1=GATE[:],
                                         op0=ALU.mult, op1=ALU.mult).then_inc(oy_ready, 1)
                dve.wait_ge(sqhi_ready, h + 1)
                dve.tensor_tensor(m_lo[:, 0:T], X1[:], m_hi[:, 0:T].bitcast(f32), ALU.subtract).then_inc(sqlo_ready, 1)

            def finish_c(h):
                dve.wait_ge(orms_ready, h + 1)
                dve.reciprocal(S[:], S[:]).then_inc(orin_ready, 1)
                dve.wait_ge(orin_ready, h + 1)
                dve.tensor_tensor(Y[:, ds(h, 1), :].rearrange("p a t -> p (a t)"), GATE[:], S[:],
                                  ALU.mult).then_inc(y_ready, 1)

            def head(i, first=False):
                if not first:
                    finish_a(i - 1)
                    split_lo(4 * i + 1, 1)
                    finish_b(i - 1)
                dve.wait_ge(fsig_ready, i + 1)
                dve.tensor_scalar(F, F, column(omlb, i), column(lb, i), ALU.mult, ALU.add).then_inc(fk_ready, 1)
                dve.wait_ge(fk_ready, 2 * i + 1)
                dve.tensor_scalar(K, F, -1.0, 1.0, ALU.mult, ALU.add).then_inc(fk_ready, 1)
                split_lo(4 * i + 2, 0)
                if not first:
                    finish_c(i - 1)
                dve.wait_ge(qsig_ready, i + 1)
                if not first:
                    dve.wait_ge(o_done, i)
                dve.tensor_tensor(Q, PJ[1][:], SIG[:], ALU.mult).then_inc(q_ready, 1)
                split_lo(4 * i + 3, 1)
                dve.wait_ge(fk_ready, 2 * i + 2)
                dve.wait_ge(lvl_done, LVLS * i + 1)
                dve.tensor_tensor(pair_half(K, 1, 0), pair_half(K, 1, 0), pair_half(F, 1, 1), ALU.mult).then_inc(tree, 1)
                masked_copy(i, 0, 0, 1)
                dve.wait_ge(at_dve, AD * i + 1)
                dve.wait_ge(lvl_done, LVLS * i + 2)
                dve.tensor_tensor(Q, Q, F, ALU.mult).then_inc(tree, 1)
                dve.wait_ge(tree, TS * i + 2)
                dve.tensor_tensor(pair_half(Q, 1, 1), pair_half(Q, 1, 1), pair_half(F, 1, 0), ALU.mult).then_inc(tree, 1)
                dve.tensor_tensor(seg_total(2), pair_half(F, 1, 0).rearrange("p n m -> p (n m)"),
                                  pair_half(F, 1, 1).rearrange("p n m -> p (n m)"), ALU.mult).then_inc(tree, 1)
                masked_copy(i, 1, 1, 1)
                for k, m in enumerate(LEVELS[:-1]):
                    dve.wait_ge(lvl_done, LVLS * i + 3 + k)
                    dve.wait_ge(tree, TS * i + 4 + 3 * k)
                    if k < 4:
                        dve.wait_ge(at_dve, AD * i + 2 + k)
                    tree_stage(i, 4 + 3 * k, m)
                    if k < 4:
                        masked_copy(i, 2 + k, 2 + k, m)
                    if k == 1:
                        split_lo(4 * i + 4, 0)

            dve.wait_ge(consts, N_CONSTS)
            head(0, first=True)
            with dve.Fori(1, HEADS) as i:
                head(i)

            steps = [0]

            def done(ins):
                ins.then_inc(pool_step, 1)
                steps[0] += 1

            def pooled(g, c, u):
                w = 2 << g
                dve.wait_ge(u_ready, 2 * g + c + 1)
                if g or c:
                    dve.wait_ge(dlo_ready, 2 * g + c)
                bufs = [Gp, Qp]
                src = u
                for k in range(g + 1):
                    dst = bufs[k % 2]
                    sh = 1 << k
                    done(dve.tensor_tensor(dst[:, PAD:], src[:, PAD:], src[:, PAD - sh:PAD + T - sh], ALU.add))
                    dve.wait_ge(pool_step, steps[0])
                    src = dst
                n = w - 1
                done(dve.tensor_tensor(fix[:, 0:n], src[:, PAD:PAD + n], rcount[:, 0:n], ALU.mult))
                dve.wait_ge(pool_step, steps[0])
                done(dve.scalar_tensor_tensor(out=Q, in0=src[:, PAD:], scalar=1.0 / w, in1=u[:, PAD:],
                                              op0=ALU.mult, op1=ALU.subtract))
                dve.wait_ge(pool_step, steps[0])
                dve.tensor_tensor(Q[:, 0:n], fix[:, 0:n], u[:, PAD:PAD + n], ALU.subtract).then_inc(pool_dd, 1)

            def low_dd(g, c):
                dve.wait_ge(dhi_ready, 2 * g + c + 1)
                dve.tensor_tensor(m_lo[:, 0:T], Q, m_hi[:, 0:T].bitcast(f32), ALU.subtract).then_inc(dlo_ready, 1)

            def first_out(g):
                dve.wait_ge(mix_done, 2 * g + 2)
                dve.wait_ge(pgate_ready, 2 * g + 1)
                dve.scalar_tensor_tensor(out=Y[:, HEADS + PT * g, :], in0=LV[:], scalar=psc[:, PT * g:PT * g + 1],
                                         in1=GATE[:], op0=ALU.mult, op1=ALU.mult).then_inc(py_ready, 1)

            def second_out(g):
                dve.wait_ge(psig_ready, 2 * g + 2)
                dve.tensor_tensor(S[:], PJ[1][:], SIG[:], ALU.mult).then_inc(pgate_ready, 1)
                dve.wait_ge(pgate_ready, 2 * g + 2)
                dve.scalar_tensor_tensor(out=Y[:, HEADS + PT * g + 1, :], in0=R[:],
                                         scalar=psc[:, PT * g + 1:PT * g + 2], in1=S[:],
                                         op0=ALU.mult, op1=ALU.mult).then_inc(py_ready, 1)

            for g in range(GROUPS):
                i = HEADS + g
                if g == 0:
                    finish_a(HEADS - 1)
                    split_lo(4 * i + 1, 1)
                    finish_b(HEADS - 1)
                else:
                    second_out(g - 1)
                    split_lo(4 * i + 1, 1)
                split_lo(4 * i + 2, 0)
                if g == 0:
                    finish_c(HEADS - 1)
                pooled(g, 0, Kp)
                dve.wait_ge(pwhi_ready, g + 1)
                dve.tensor_tensor(m_lo[:, T:], X1[:, 0:2 * PT * P], m_hi[:, T:].bitcast(f32),
                                  ALU.subtract).then_inc(pwlo_ready, 1)
                low_dd(g, 0)
                split_lo(4 * i + 3, 1)
                pooled(g, 1, Fp)
                dve.wait_ge(mix_done, 2 * g + 1)
                low_dd(g, 1)
                dve.wait_ge(psig_ready, 2 * g + 1)
                if g == 0:
                    dve.wait_ge(y_ready, HEADS)
                else:
                    dve.wait_ge(py_ready, 2 * g)
                dve.tensor_tensor(GATE[:], PJ[0][:], SIG[:], ALU.mult).then_inc(pgate_ready, 1)
                split_lo(4 * i + 4, 0)
                first_out(g)

            def y_lo(o, j, slot):
                cols = slice(slot * HALF, (slot + 1) * HALF)
                dve.wait_ge(yhi_ready, SLOTS * o + j + 1)
                dve.tensor_tensor(m_lo[:, cols].rearrange("p (a n) -> p a n", a=1),
                                  Y[:, ds(j, 1), o * HALF:(o + 1) * HALF],
                                  m_hi[:, cols].bitcast(f32).rearrange("p (a n) -> p a n", a=1),
                                  ALU.subtract).then_inc(ylo_ready, 1)

            def out_pair(o, j):
                n = UNITS + SLOTS * o + 2 * j
                y_lo(o, 2 * j, 0)
                split_lo(n + 1, 1)
                y_lo(o, 2 * j + 1, 1)
                split_lo(n + 2, 0)

            def residual(n):
                t = n % OT
                if t < OT - 1 or n == TT - 1:
                    dve.wait_ge(tile_done, (OT - 1) * (n // OT) + t + 1)
                else:
                    dve.wait_ge(unit_done, UNITS + SLOTS * (n // OT + 1))
                dve.wait_ge(xres_loaded[t], 16 * (n // OT) + 16)
                if n >= OT:
                    dve.wait_ge(early_stored[t], 16 * (n // OT))
                dve.tensor_tensor(RES[t], BANKS[t][:], (Q, K, F, G)[t], ALU.add).then_inc(res_ready, 1)

            def finish_tile(n):
                t = n % OT
                dve.wait_ge(frms_ready, n + 1)
                dve.reciprocal(rin[:, n:n + 1], rms[:, n:n + 1]).then_inc(frin_ready, 1)
                dve.wait_ge(frin_ready, n + 1)
                dve.wait_ge(gfin_loaded, 16)
                dve.scalar_tensor_tensor(out=RES[t], in0=RES[t], scalar=rin[:, n:n + 1], in1=V[:],
                                         op0=ALU.mult, op1=ALU.mult).then_inc(fin_ready, 1)

            for o in range(OG):
                n = UNITS + SLOTS * o
                if o == 0:
                    y_lo(0, 0, 0)
                    second_out(GROUPS - 1)
                    split_lo(n + 1, 1)
                    y_lo(0, 1, 1)
                    split_lo(n + 2, 0)
                else:
                    n0 = OT * (o - 1)
                    y_lo(o, 0, 0)
                    residual(n0)
                    residual(n0 + 1)
                    residual(n0 + 2)
                    split_lo(n + 1, 1)
                    residual(n0 + 3)
                    y_lo(o, 1, 1)
                    split_lo(n + 2, 0)
                    finish_tile(n0)
                    y_lo(o, 2, 0)
                    split_lo(n + 3, 1)
                    finish_tile(n0 + 1)
                    y_lo(o, 3, 1)
                    split_lo(n + 4, 0)
                    finish_tile(n0 + 2)
                    finish_tile(n0 + 3)
                with dve.Fori(1 if o == 0 else 2, SLOTS // 2 - 1) as j:
                    out_pair(o, j)
                if o < OG - 1:
                    out_pair(o, SLOTS // 2 - 1)
            y_lo(OG - 1, SLOTS - 2, 0)
            split_lo(UNITS + SLOTS * OG - 1, 1)
            y_lo(OG - 1, SLOTS - 1, 1)
            n0 = OT * (OG - 1)
            for t in range(OT):
                residual(n0 + t)
                if t:
                    finish_tile(n0 + t - 1)
            finish_tile(n0 + OT - 1)

        @block.tensor
        def _(pe):
            def steps(slot, lo, hi, halves=range(NH)):
                for k in range(lo, hi):
                    cols = slice(k * P, (k + 1) * P)
                    for a, b, first, last in ((w_hi, h_hi, True, False), (w_hi, h_lo, False, False),
                                              (w_lo, h_hi, False, True)):
                        for h in halves:
                            mm = pe.matmul(PJ[slot][:, h * HALF:(h + 1) * HALF], a[:, slot, cols],
                                           b[:, k, h * HALF:(h + 1) * HALF],
                                           start=(k == 0 and first), stop=(k == KT - 1 and last),
                                           skip_group_check=True)
                if hi == KT and halves[-1] == NH - 1:
                    mm.then_inc(unit_done, 1)

            def chunk(b, c):
                return b[:, c * C:(c + 1) * C]

            def level(h, j):
                if j < 2:
                    if not (isinstance(h, int) and h == 0):
                        pe.wait_ge(orms_ready, h)
                else:
                    pe.wait_ge(at_dve, AD * h + j - 1)
                if j == 0:
                    pe.wait_ge(q_ready, h + 1)
                    m, which = 1, 0
                elif j == 1:
                    pe.wait_ge(tree, TS * h + 1)
                    m, which = 1, 1
                else:
                    pe.wait_ge(tree, TS * h + 4 + 3 * (j - 2))
                    m, which = LEVELS[j - 2], 1
                for c in range(TT):
                    for s in range(0, C, B):
                        if 2 * m <= B:
                            t, n = s, B
                        elif s % (2 * m) < m:
                            t, n = s - s % (2 * m), 2 * m
                        else:
                            continue
                        queries = pair_half(Q[:, c * C + t:c * C + t + n], m, which)
                        mm = pe.matmul(lv(j)[s:s + B, c * HC + t // 2:c * HC + (t + n) // 2],
                                       K[:, c * C + s:c * C + s + B], queries, start=True, stop=True)
                mm.then_inc(lvl_done, 1)

            def v_transposes(h):
                pe.wait_ge(vT_ready, h + 1)
                if not (isinstance(h, int) and h == 0):
                    pe.wait_ge(oy_ready, h)
                for c in range(TT):
                    mm = pe.transpose(chunk(R, c), chunk(X1, c), ident[:])
                mm.then_inc(vtr_done, 1)

            def k_transposes(h):
                pe.wait_ge(tree, TS * h + TS)
                pe.wait_ge(v_ready, h + 1)
                for c in range(TT):
                    mm = pe.transpose(chunk(R, c), chunk(K, c), ident[:])
                mm.then_inc(kdtr_done, 1)

            def outer_products(h):
                pe.wait_ge(kd_ready, h + 1)
                for c in range(TT):
                    mm = pe.matmul(chunk(R, c), chunk(X1, c), chunk(V, c), start=True, stop=True)
                mm.then_inc(kv_done, 1)

            def readout(h):
                pe.wait_ge(at_dve, AD * h + AD)
                pe.wait_ge(at_act, AA * h + AA)
                pe.wait_ge(state, (TT - 1) * (h + 1))
                for c in range(TT):
                    mm = pe.matmul(chunk(R, c), chunk(V, c), AT[:, c, :], start=True, stop=(c == 0))
                    if c:
                        mm = pe.matmul(chunk(R, c), chunk(S, c), chunk(Q, c), start=False, stop=True)
                mm.then_inc(o_done, 1)

            def means(h):
                pe.wait_ge(sqlo_ready, h + 1)
                for k in range(NH):
                    tok = slice(k * HALF, (k + 1) * HALF)
                    pe.matmul(LV[:, tok], mean_w[:], m_hi[:, tok], start=True, stop=False)
                    mm = pe.matmul(LV[:, tok], mean_w[:], m_lo[:, tok], start=False, stop=True)
                mm.then_inc(mean_done, 1)

            def x_transposes(t):
                pe.wait_ge(xn_ready, t + 1)
                if t >= 2:
                    pe.wait_ge(hlo_ready, t - 1)
                for k in range(KT):
                    mm = pe.transpose(XT[t % 2][:, k * P:(k + 1) * P],
                                      Y[:, SLOTS - TT + t, k * P:(k + 1) * P], ident[:])
                mm.then_inc(xT_ready, 1)

            def first_units():
                pe.wait_ge(ident_ready, 1)
                for t in range(TT // 2 + 1):
                    x_transposes(t)
                pe.wait_ge(wlo_ready, 1)
                pe.wait_ge(hlo_ready, TT // 2)
                steps(0, 0, 4, [0])
                x_transposes(5)
                steps(0, 4, 8, [0])
                x_transposes(6)
                pe.wait_ge(wlo_ready, 2)
                steps(1, 0, 4, [0])
                x_transposes(7)
                steps(1, 4, 8, [0])
                pe.wait_ge(hlo_ready, TT)
                for slot in range(2):
                    steps(slot, 0, KT, [1])

            def units_01(i, finished):
                pe.wait_ge(wlo_ready, 4 * i + 1)
                pe.wait_ge(vT_ready, finished + 1)
                steps(0, 0, 2)
                k_transposes(finished)
                steps(0, 2, 4)
                outer_products(finished)
                steps(0, 4, 7)
                readout(finished)
                steps(0, 7, 8)
                pe.wait_ge(wlo_ready, 4 * i + 2)
                pe.wait_ge(gate_ready, finished + 1)
                steps(1, 0, 2)
                means(finished)
                steps(1, 2, 8)

            def head(i, first=False):
                if first:
                    first_units()
                else:
                    units_01(i, i - 1)
                pe.wait_ge(wlo_ready, 4 * i + 3)
                pe.wait_ge(fsig_ready, i + 1)
                steps(0, 0, 2)
                level(i, 0)
                steps(0, 2, 3)
                level(i, 1)
                steps(0, 3, 6)
                level(i, 2)
                steps(0, 6, 8)
                pe.wait_ge(wlo_ready, 4 * i + 4)
                pe.wait_ge(q_ready, i + 1)
                level(i, 3)
                steps(1, 0, 2)
                level(i, 4)
                steps(1, 2, 3)
                v_transposes(i)
                steps(1, 3, 4)
                level(i, 5)
                steps(1, 4, 6)
                level(i, 6)
                steps(1, 6, 8)
                level(i, 7)

            head(0, first=True)
            with pe.Fori(1, HEADS) as i:
                head(i)

            def mix(g, c):
                pe.wait_ge(dlo_ready, 2 * g + c + 1)
                if c == 0:
                    pe.wait_ge(pwlo_ready, g + 1)
                for d, dst in enumerate((LV, R)):
                    cols = slice(T + c * PT * P + d * P, T + c * PT * P + (d + 1) * P)
                    for h in range(NH):
                        tok = slice(h * HALF, (h + 1) * HALF)
                        for k, (a, b) in enumerate(((m_hi, m_hi), (m_hi, m_lo), (m_lo, m_hi))):
                            mm = pe.matmul(dst[:, tok], a[:, cols], b[:, tok], start=(c == 0 and k == 0),
                                           stop=(c == PT - 1 and k == 2), skip_group_check=True)
                mm.then_inc(mix_done, 1)

            def group(g, first=False):
                i = g + HEADS
                if first:
                    units_01(i, HEADS - 1)
                else:
                    pe.wait_ge(wlo_ready, 4 * i + 1)
                    pe.wait_ge(pgate_ready, 2 * g - 1)
                    steps(0, 0, KT)
                    pe.wait_ge(wlo_ready, 4 * i + 2)
                    pe.wait_ge(pgate_ready, 2 * g)
                    steps(1, 0, KT)
                pe.wait_ge(wlo_ready, 4 * i + 3)
                pe.wait_ge(u_ready, 2 * g + 1)
                steps(0, 0, 3)
                if first:
                    pe.wait_ge(y_ready, HEADS)
                else:
                    pe.wait_ge(py_ready, 2 * g)
                mix(g, 0)
                steps(0, 3, 8)
                pe.wait_ge(wlo_ready, 4 * i + 4)
                pe.wait_ge(u_ready, 2 * g + 2)
                steps(1, 0, 4)
                mix(g, 1)
                steps(1, 4, 8)

            group(0, first=True)
            with pe.Fori(1, GROUPS) as g:
                group(g)

            def out_tile(t, slot, first, last):
                tok = slice(slot * HALF + t * P, slot * HALF + (t + 1) * P)
                for k, (a, b) in enumerate(((m_hi, w_hi), (m_hi, w_lo), (m_lo, w_hi))):
                    for h in range(D // HALF):
                        cols = slice(h * HALF, (h + 1) * HALF)
                        mm = pe.matmul(BANKS[t][:, cols], a[:, tok], b[:, slot, cols],
                                       start=(first and k == 0), stop=(last and k == 2),
                                       skip_group_check=True)
                return mm

            def bank_free(o, t):
                if o:
                    pe.wait_ge(res_ready, OT * (o - 1) + t + 1)
                else:
                    pe.wait_ge(*((pgate_ready, 2 * GROUPS - 1), (py_ready, 2 * GROUPS - 1),
                                 (pgate_ready, 2 * GROUPS), (py_ready, 2 * GROUPS))[t])

            def out_unit(o, n, slot, first=False, last=False):
                pe.wait_ge(wlo_ready, n + 1)
                pe.wait_ge(ylo_ready, n - UNITS + 1)
                for t in range(OT):
                    if first:
                        bank_free(o, t)
                    mm = out_tile(t, slot, first, last)
                    if last and t < OT - 1:
                        mm.then_inc(tile_done, 1)
                mm.then_inc(unit_done, 1)

            for o in range(OG):
                n0 = UNITS + SLOTS * o
                out_unit(o, n0, 0, first=True)
                out_unit(o, n0 + 1, 1)
                with pe.Fori(1, SLOTS // 2 - 1) as j:
                    out_unit(o, n0 + 2 * j, 0)
                    out_unit(o, n0 + 2 * j + 1, 1)
                if o < OG - 1:
                    out_unit(o, n0 + SLOTS - 2, 0)
                    out_unit(o, n0 + SLOTS - 1, 1, last=True)
            pe.wait_ge(wlo_ready, UNITS + SLOTS * OG - 1)
            pe.wait_ge(ylo_ready, SLOTS * OG - 1)
            for t in range(OT - 1):
                out_tile(t, 0, False, False)
            pe.wait_ge(wlo_ready, UNITS + SLOTS * OG)
            pe.wait_ge(ylo_ready, SLOTS * OG)
            for t in range(OT - 1):
                out_tile(t, 1, False, True).then_inc(tile_done, 1)
            out_tile(OT - 1, 0, False, False)
            out_tile(OT - 1, 1, False, True).then_inc(tile_done, 1)


_INS = ['x', 'norm1_g', 'w_in', 'pool_w', 'pool_scale', 'lb_logits', 'rec_norm_g', 'w_out', 'final_norm_g']


def kernel(**inputs):
    import numpy as _np
    import concourse.bacc as _bacc
    from concourse import mybir as _mybir
    from concourse.bass_utils import run_bass_kernel_spmd as _run

    nc = _bacc.Bacc("TRN2", target_bir_lowering=False, num_devices=1)
    arrays, args = {}, []
    for name in _INS:
        a = _np.ascontiguousarray(inputs[name])
        arrays[f"in_{name}_dram"] = a
        args.append(nc.dram_tensor(f"in_{name}_dram", a.shape, _mybir.dt.from_np(a.dtype), kind="ExternalInput").ap())
    shape = inputs["x"].shape
    args.append(nc.dram_tensor("out_0_dram", shape, _mybir.dt.float32, kind="ExternalOutput").ap())
    hybrid_pool_hgrn2_kernel(nc, *args)
    r = _run(nc, [arrays], core_ids=[0])
    return r.results[0]["out_0_dram"]
```

```python
import concourse.bass as bass
from concourse import mybir
from contextlib import ExitStack


def hybrid_pool_hgrn2_kernel(nc, x, norm1_g, w_in, pool_w, pool_scale, lb_logits,
                             rec_norm_g, w_out, final_norm_g, out):
    f32 = mybir.dt.float32
    f32r = mybir.dt.float32r
    u32 = mybir.dt.uint32
    ALU = mybir.AluOpType
    ACT = mybir.ActivationFunctionType
    ds = bass.ds

    P = 128
    T, D = x.shape[1], x.shape[2]
    KT = D // P
    TT = T // P
    HALF = 512
    NH = T // HALF
    C = P
    HC = C // 2
    B = 32
    VAR = 3 * B // 2
    HEADS = D // P
    GROUPS = pool_w.shape[1]
    PT = D // GROUPS // P
    EPS = 1e-6
    PAD = 16
    BLOCKS = HEADS + GROUPS
    UNITS = 4 * BLOCKS
    SLOTS = HEADS + PT * GROUPS
    OG = 2
    OT = TT // OG

    POOL_IN, POOL_GATE, QC, FC, VC, GC = (k * D for k in range(6))

    w_in_v = w_in[0].rearrange("(k p) n -> p k n", p=P)
    w_out_v = w_out[0].rearrange("(s p) n -> p s n", p=P)
    pool_w_v = pool_w[0].rearrange("g (c p) n -> g p c n", p=P)
    x_v = x[0].rearrange("(t p) d -> t p d", p=P)
    out_v = out[0].rearrange("(t p) d -> t p d", p=P)

    ctx = ExitStack()
    with ctx:
        def sb(name, shape, dt=f32):
            return ctx.enter_context(nc.sbuf_tensor(name, shape, dt))

        def sem(name):
            return ctx.enter_context(nc.semaphore(name))

        h_hi = sb("h_hi", [P, KT, T], f32r)
        h_lo = sb("h_lo", [P, KT, T], f32r)
        Y = sb("Y", [P, SLOTS, T])
        w_raw = sb("w_raw", [P, 2, KT * P])
        w_hi = sb("w_hi", [P, 2, KT * P], f32r)
        w_lo = sb("w_lo", [P, 2, KT * P], f32r)
        m_hi = sb("m_hi", [P, T + 2 * PT * P], f32r)
        m_lo = sb("m_lo", [P, T + 2 * PT * P], f32r)
        Qp = sb("Qp", [P, PAD + T])
        Kp = sb("Kp", [P, PAD + T])
        Fp = sb("Fp", [P, PAD + T])
        Gp = sb("Gp", [P, PAD + T])
        Q, K, F, G = (b[:, PAD:PAD + T] for b in (Qp, Kp, Fp, Gp))
        V = sb("V", [P, T])
        X1 = sb("X1", [P, T])
        AT = sb("AT", [P, TT, C])
        AB = sb("AB", [P, TT, B])
        GS = sb("GS", [P, 2 * T])
        GATE = GS[:, 0:T]
        S = GS[:, T:2 * T]
        QV = GS[:, 0:T // B * VAR]
        SIG = sb("SIG", [P, T])

        ident = sb("ident", [P, P])
        mean_w = sb("mean_w", [P, P], f32r)
        masks = sb("masks", [P, 3, VAR])
        rcount = sb("rcount", [P, PAD])
        fix = sb("fix", [P, PAD])
        eps = sb("eps", [P, 1])
        warm = sb("warm", [P, 1])
        lbl = sb("lbl", [P, 2, HEADS])
        lbm = sb("lbm", [P, HEADS])
        lb = sb("lb", [P, HEADS])
        omlb = sb("omlb", [P, HEADS])
        rg = sb("rg", [P, HEADS])
        psc = sb("psc", [P, HEADS])
        ss = sb("ss", [P, TT + 1])
        rms = sb("rms", [P, TT])
        rin = sb("rin", [P, TT])

        PJ = [ctx.enter_context(nc.psum_tensor(f"PJ{i}", [P, T], f32)) for i in range(2)]
        LV = ctx.enter_context(nc.psum_tensor("LV", [P, T], f32))
        R = ctx.enter_context(nc.psum_tensor("R", [P, T], f32))
        BANKS = [PJ[0], LV, PJ[1], R]
        XT = [LV, R]

        x_loaded = [sem(f"x_loaded{t}") for t in range(TT)]
        params_loaded = sem("params_loaded")
        grow_loaded = sem("grow_loaded")
        w_loaded = [sem(f"w_loaded{i}") for i in range(2)]
        pw_loaded = sem("pw_loaded")
        xres_loaded = [sem(f"xres_loaded{t}") for t in range(OT)]
        gfin_loaded = sem("gfin_loaded")
        early_stored = [sem(f"early_stored{t}") for t in range(OT)]
        out_stored = [sem(f"out_stored{t}") for t in range(OT)]
        eps_ready = sem("eps_ready")
        ident_ready = sem("ident_ready")
        consts = sem("consts")
        const_step = sem("const_step")
        ss_ready = sem("ss_ready")
        rms_ready = sem("rms_ready")
        rin_ready = sem("rin_ready")
        xn_ready = sem("xn_ready")
        xT_ready = sem("xT_ready")
        hhi_ready = sem("hhi_ready")
        hlo_ready = sem("hlo_ready")
        lb_step = sem("lb_step")
        lb_exp = sem("lb_exp")
        whi_ready = sem("whi_ready")
        wlo_ready = sem("wlo_ready")
        unit_done = sem("unit_done")
        fsig_ready = sem("fsig_ready")
        qsig_ready = sem("qsig_ready")
        gsig_ready = sem("gsig_ready")
        vb_ready = sem("vb_ready")
        v_ready = sem("v_ready")
        kb_ready = sem("kb_ready")
        kd_act = sem("kd_act")
        kd_dve = sem("kd_dve")
        sq_ready = sem("sq_ready")
        sqhi_ready = sem("sqhi_ready")
        sqlo_ready = sem("sqlo_ready")
        orms_ready = sem("orms_ready")
        at_act = sem("at_act")
        at_dve = sem("at_dve")
        fk_ready = sem("fk_ready")
        q_ready = sem("q_ready")
        tree = sem("tree")
        state = sem("state")
        gate_ready = sem("gate_ready")
        oy_ready = sem("oy_ready")
        orin_ready = sem("orin_ready")
        y_ready = sem("y_ready")
        qv_act = sem("qv_act")
        qv_dve = sem("qv_dve")
        lvl_done = sem("lvl_done")
        kv_done = sem("kv_done")
        o_done = sem("o_done")
        mean_done = sem("mean_done")
        u_ready = sem("u_ready")
        pool_step = sem("pool_step")
        pool_dd = sem("pool_dd")
        dhi_ready = sem("dhi_ready")
        dlo_ready = sem("dlo_ready")
        pwhi_ready = sem("pwhi_ready")
        pwlo_ready = sem("pwlo_ready")
        psig_ready = sem("psig_ready")
        pgate_ready = sem("pgate_ready")
        mix_done = sem("mix_done")
        py_ready = sem("py_ready")
        yhi_ready = sem("yhi_ready")
        ylo_ready = sem("ylo_ready")
        tile_done = sem("tile_done")
        res_ready = sem("res_ready")
        fss_ready = sem("fss_ready")
        bias_ready = sem("bias_ready")
        frms_ready = sem("frms_ready")
        frin_ready = sem("frin_ready")
        fin_ready = sem("fin_ready")

        LEVELS = [2, 4, 8, 16, 32, 64]
        STAGES = 5
        TS = 4 + 3 * len(LEVELS)
        AD = 2 + 3 + 3
        AA = C // B + 3
        BM = (C // B) * (P // B)
        GOFF = {2: 0}
        for m in LEVELS:
            GOFF[2 * m] = GOFF[m] + T // m

        def seg_total(m):
            return F if m == 1 else G[:, GOFF[m]:GOFF[m] + T // m]

        def pair_half(b, m, which):
            return b.rearrange("p (n two m) -> p n two m", two=2, m=m)[:, :, which, :]

        def block_at(b, row, col, chunks):
            return b[row:row + B, 0:chunks * P].rearrange("p (c n) -> p c n", n=P)[:, :, col:col + B]

        def lv(j):
            return LV[:, (j % 2) * HALF:(j % 2 + 1) * HALF]

        block = ctx.enter_context(nc.Block())

        N_CONSTS = 3 + 4 + PAD
        RES = [AT[:].rearrange("p c t -> p (c t)"), GATE, S, SIG[:]]

        @block.gpsimd
        def _(pool):
            pool.memset(eps[:], EPS).then_inc(eps_ready, 1)
            pool.memset(ident[:], 0.0).then_inc(const_step, 1)
            pool.wait_ge(const_step, 1)
            pool.affine_select(out=ident[:], in_=ident[:], compare_op=ALU.not_equal, fill=1.0, base=0,
                               pattern=[[-1, P]], channel_multiplier=1).then_inc(ident_ready, 1)
            full = AT[:].rearrange("p c t -> p (c t)")
            pool.memset(full, 1.0).then_inc(const_step, 1)
            pool.wait_ge(const_step, 2)
            NB = C // B
            W = NB * VAR
            parts = [(full[:, 2 * W:2 * W + HC], [[-2, HC]], 1)]
            for k, m in enumerate((2, 8)):
                v = full[:, k * W:(k + 1) * W].rearrange("p (n s m) -> p n s m", s=6, m=m)
                parts += [(v[:, :, 0:3, :], [[-4 * m, C // (4 * m)], [-m, 3], [0, m]], m),
                          (v[:, :, 3:5, :], [[-4 * m, C // (4 * m)], [-m, 2], [0, m]], m),
                          (v[:, :, 5, :], [[-4 * m, C // (4 * m)], [0, m]], m)]
            for v, pattern, width in parts:
                pool.affine_select(out=v, in_=v, compare_op=ALU.is_ge, fill=0.0, base=0,
                                   pattern=pattern, channel_multiplier=1).then_inc(const_step, 1)
            pool.wait_ge(const_step, 2 + len(parts))
            for v, pattern, width in parts:
                pool.affine_select(out=v, in_=v, compare_op=ALU.is_ge, fill=0.0, base=width - 1,
                                   pattern=[[-step, n] for step, n in pattern],
                                   channel_multiplier=-1).then_inc(const_step, 1)
            pool.wait_ge(const_step, 2 + 2 * len(parts))
            done = 2 + 2 * len(parts)
            sums = [(masks[:, 0, 0:B], ident[:], B), (masks[:, 0, B:VAR], full[:, 2 * W:2 * W + HC], VAR - B),
                    (masks[:, 1, :], full[:, 0:W], VAR), (masks[:, 2, :], full[:, W:2 * W], VAR)]
            for b in range(1, NB):
                for dst, src, n in sums:
                    pool.tensor_tensor(dst, src[:, 0:n] if b == 1 else dst, src[:, b * n:(b + 1) * n],
                                       ALU.add).then_inc(const_step, 1)
                done += len(sums)
                pool.wait_ge(const_step, done)
            pool.memset(AB[:], 0.0).then_inc(consts, 1)
            pool.memset(mean_w[:].bitcast(f32), 1.0 / P).then_inc(consts, 1)
            pool.memset(AT[:], 0.0).then_inc(consts, 1)
            for b in (Qp, Kp, Fp, Gp):
                pool.memset(b[:, 0:PAD], 0.0).then_inc(consts, 1)
            for t in range(PAD):
                pool.memset(rcount[:, t:t + 1], 1.0 / (t + 1)).then_inc(consts, 1)
            for n in range(TT - OT):
                pool.wait_ge(fin_ready, n + 1)
                pool.dma_start(out_v[n], RES[n % OT]).then_inc(early_stored[n % OT], 16)
            for t in range(OT):
                pool.wait_ge(early_stored[t], 16 * (OG - 1))

        @block.sync
        def _(sp):
            def load_unit(n, slot, src, first=False):
                if not first:
                    sp.wait_ge(wlo_ready, n - 1)
                sp.dma_start(w_raw[:, slot, :].rearrange("p (k n) -> p k n", n=P), src).then_inc(w_loaded[slot], 16)

            def load_head_unit(i, u, first=False):
                load_unit(4 * i + u, u % 2, w_in_v[:, :, ds((FC, QC, VC, GC)[u] + i * P, P)], first)

            def load_group(g):
                for u, (base, c) in enumerate(((POOL_IN, 0), (POOL_IN, 1), (POOL_GATE, 0), (POOL_GATE, 1))):
                    load_unit(4 * (HEADS + g) + u, u % 2, w_in_v[:, :, ds(base + c * P + g * (PT * P), P)])

            def load_pool_w(g):
                if isinstance(g, int) and g == 0:
                    sp.wait_ge(mean_done, HEADS)
                else:
                    sp.wait_ge(pwlo_ready, g)
                sp.dma_start(X1[:, 0:2 * PT * P].rearrange("p (a c n) -> p a c n", a=1, c=PT),
                             pool_w_v[ds(g, 1)].rearrange("a p c n -> p a c n")).then_inc(pw_loaded, 16)

            def load_out_pair(n, row):
                for u in range(2):
                    sp.wait_ge(wlo_ready, n + u - 1)
                    sp.dma_start(w_raw[:, u, :].rearrange("p (a n) -> p a n", a=1),
                                 w_out_v[:, ds(row + u, 1), :]).then_inc(w_loaded[u], 16)

            for t in range(TT):
                sp.dma_start(Y[:, SLOTS - TT + t, :], x_v[t]).then_inc(x_loaded[t], 16)
                if t == 2 or t == 3:
                    load_head_unit(0, t - 2, first=True)
            for u in range(2, 4):
                load_head_unit(0, u)
            with sp.Fori(1, HEADS) as i:
                for u in range(4):
                    load_head_unit(i, u)
            load_group(0)
            load_pool_w(0)
            with sp.Fori(1, GROUPS) as g:
                load_group(g)
                load_pool_w(g)
            for o in range(OG):
                n0 = UNITS + SLOTS * o
                with sp.Fori(0, HEADS // 2) as j:
                    load_out_pair(n0 + 2 * j, (SLOTS - HEADS) + 2 * j)
                if o == 0:
                    sp.wait_ge(py_ready, PT * GROUPS)
                    sp.dma_start(V[:], final_norm_g.partition_broadcast(P)).then_inc(gfin_loaded, 16)
                for t, b in enumerate((Q, K, F, G)):
                    if o:
                        sp.wait_ge(res_ready, OT * (o - 1) + t + 1)
                    sp.dma_start(b, x_v[OT * o + t]).then_inc(xres_loaded[t], 16)
                with sp.Fori(0, (SLOTS - HEADS) // 2) as j:
                    load_out_pair(n0 + HEADS + 2 * j, 2 * j)

            for t in range(OT - 1):
                sp.wait_ge(fin_ready, TT - OT + t + 1)
                sp.dma_start(out_v[TT - OT + t], RES[t]).then_inc(out_stored[t], 16)
            for h in range(2):
                cols = slice(h * HALF, (h + 1) * HALF)
                sp.wait_ge(fin_ready, TT + h)
                sp.dma_start(out_v[TT - 1][:, cols], RES[OT - 1][:, cols]).then_inc(out_stored[OT - 1], 16)
            for t in range(OT):
                sp.wait_ge(out_stored[t], 16 if t < OT - 1 else 32)

        @block.scalar
        def _(act):
            def split_hi(half_n, slot):
                act.wait_ge(w_loaded[slot], half_n * 16 + 16)
                if not (isinstance(half_n, int) and half_n == 0):
                    act.wait_ge(unit_done, half_n * 2 + slot - 1)
                act.activation(w_hi[:, slot, :], w_raw[:, slot, :], ACT.Copy).then_inc(whi_ready, 1)

            act.dma_start(S, norm1_g.partition_broadcast(P)).then_inc(grow_loaded, 16)

            def token_rms(t):
                act.wait_ge(x_loaded[t], 16)
                if t:
                    act.wait_ge(ss_ready, t)
                act.activation(X1[:], Y[:, SLOTS - TT + t, :], ACT.Square,
                               accum_out=ss[:, t:t + 1]).then_inc(ss_ready, 1)
                act.wait_ge(ss_ready, t + 1)
                act.activation(rms[:, t:t + 1], ss[:, t:t + 1], ACT.Sqrt, bias=eps[:, 0:1],
                               scale=1.0 / D).then_inc(rms_ready, 1)

            def high_h(t):
                act.wait_ge(xT_ready, t + 1)
                act.activation(h_hi[:, :, t * P:(t + 1) * P], XT[t % 2][:].rearrange("p (k n) -> p k n", n=P),
                               ACT.Copy).then_inc(hhi_ready, 1)

            act.wait_ge(eps_ready, 1)
            act.activation(rms[:, 0:1], eps[:, 0:1], ACT.Sqrt).then_inc(rms_ready, 1)
            act.wait_ge(rms_ready, 1)
            token_rms(0)
            token_rms(1)
            with nc.allow_non_contiguous_dma("parameters of 4 KB, transposed by the load"):
                act.dma_start(lbl[:], lb_logits.rearrange("l (h p) -> p l h", p=P)).then_inc(params_loaded, 16)
                act.dma_start(rg[:], rec_norm_g[0].rearrange("(h p) -> p h", p=P)).then_inc(params_loaded, 16)
                act.dma_start(psc[:], pool_scale[0].rearrange("(h p) -> p h", p=P)).then_inc(params_loaded, 16)
            for t in range(TT):
                high_h(t)
                if t + 2 < TT:
                    token_rms(t + 2)
                if t < 2:
                    split_hi(0, t)

            act.wait_ge(lb_step, 3)
            act.activation(lbl[:], lbl[:], ACT.Exp).then_inc(lb_exp, 1)
            act.activation(warm[:], eps[:, 0:1], ACT.Sigmoid).then_inc(lb_exp, 1)

            def copy_level(h, j, m):
                act.wait_ge(lvl_done, STAGES * h + j + 1)
                for n in range(HC // m):
                    rows = slice(2 * m * n, 2 * m * n + m)
                    act.activation(AT[rows, :, 2 * m * n + m:2 * m * n + 2 * m],
                                   lv(j).rearrange("p (c t) -> p c t", t=HC)[rows, :, m * n:m * n + m],
                                   ACT.Copy).then_inc(at_act, 1)

            def move_values(h):
                act.wait_ge(vb_ready, h + 1)
                for d in range(0, P, B):
                    for s in range(0, C, B):
                        act.activation(block_at(V, s, d, TT), block_at(X1, d, s, TT), ACT.Copy).then_inc(v_ready, 1)

            def move_keys(h):
                act.wait_ge(kb_ready, h + 1)
                act.wait_ge(v_ready, BM * h + BM)
                for d in range(0, P // 2, B):
                    for s in range(0, C, B):
                        act.activation(block_at(X1, s, d, TT - 1), block_at(S, d, s, TT - 1),
                                       ACT.Copy).then_inc(kd_act, 1)

            def copy_diagonal(h):
                act.wait_ge(at_dve, AD * h + AD)
                for s in range(0, C, B):
                    act.activation(AT[s:s + B, :, s:s + B], AB[s:s + B, :, :], ACT.Copy).then_inc(at_act, 1)

            def copy_queries(h, k, m):
                act.wait_ge(lvl_done, STAGES * h + k)
                act.wait_ge(tree, TS * h + (2 if k == 1 else 7))
                act.activation(QV.rearrange("p (n s m) -> p n s m", s=6, m=m)[:, :, 0:3, :],
                               Q.rearrange("p (n s m) -> p n s m", s=4, m=m)[:, :, 1:4, :],
                               ACT.Copy).then_inc(qv_act, 1)

            def finish_a(h):
                copy_level(h, 4, 64)
                move_keys(h)
                act.wait_ge(unit_done, 4 * h + 4)
                act.wait_ge(q_ready, h + 1)
                act.activation(SIG[:], PJ[1][:], ACT.Sigmoid).then_inc(gsig_ready, 1)

            def finish_b(h):
                act.wait_ge(o_done, h + 1)
                act.activation(X1[:], R[:], ACT.Square).then_inc(sq_ready, 1)
                act.wait_ge(sq_ready, h + 1)
                act.activation(m_hi[:, 0:T], X1[:], ACT.Copy).then_inc(sqhi_ready, 1)

            def finish_c(h):
                act.wait_ge(mean_done, h + 1)
                act.activation(S, LV[:], ACT.Sqrt, bias=eps[:, 0:1]).then_inc(orms_ready, 1)

            def head(i, first=False):
                if not first:
                    finish_a(i - 1)
                    split_hi(2 * i, 1)
                    finish_b(i - 1)
                else:
                    split_hi(1, 0)
                act.wait_ge(unit_done, 4 * i + 1)
                if not first:
                    act.wait_ge(tree, TS * (i - 1) + 4)
                act.activation(F, PJ[0][:], ACT.Sigmoid).then_inc(fsig_ready, 1)
                if not first:
                    split_hi(2 * i + 1, 0)
                    finish_c(i - 1)
                act.wait_ge(unit_done, 4 * i + 2)
                if not first:
                    act.wait_ge(gate_ready, i)
                act.activation(SIG[:], PJ[1][:], ACT.Sigmoid).then_inc(qsig_ready, 1)
                split_hi(2 * i + 1, 1)
                act.wait_ge(tree, TS * i + 1)
                act.activation(QV.rearrange("p (n x) -> p n x", x=VAR)[:, :, B:VAR],
                               Q.rearrange("p (n j two) -> p n j two", n=T // B, two=2)[:, :, :, 1],
                               ACT.Copy).then_inc(qv_act, 1)
                copy_queries(i, 1, 2)
                split_hi(2 * i + 2, 0)
                copy_queries(i, 2, 8)
                move_values(i)
                copy_diagonal(i)
                copy_level(i, 3, 32)

            act.wait_ge(consts, N_CONSTS)
            head(0, first=True)
            with act.Fori(1, HEADS) as i:
                head(i)

            def second_gate(g):
                act.wait_ge(unit_done, 4 * (HEADS + g) + 4)
                act.wait_ge(pgate_ready, 2 * g + 1)
                act.activation(SIG[:], PJ[1][:], ACT.Sigmoid).then_inc(psig_ready, 1)

            def group(g, first=False):
                i = g + HEADS
                if first:
                    finish_a(HEADS - 1)
                else:
                    second_gate(g - 1)
                split_hi(2 * i, 1)
                if first:
                    finish_b(HEADS - 1)
                act.wait_ge(unit_done, 4 * i + 1)
                act.activation(K, PJ[0][:], ACT.Copy).then_inc(u_ready, 1)
                split_hi(2 * i + 1, 0)
                if first:
                    finish_c(HEADS - 1)
                act.wait_ge(pw_loaded, 16 * g + 16)
                if not first:
                    act.wait_ge(mix_done, 2 * g)
                act.activation(m_hi[:, T:], X1[:, 0:2 * PT * P], ACT.Copy).then_inc(pwhi_ready, 1)
                act.wait_ge(pool_dd, 2 * g + 1)
                act.activation(m_hi[:, 0:T], Q, ACT.Copy).then_inc(dhi_ready, 1)
                act.wait_ge(unit_done, 4 * i + 2)
                act.activation(F, PJ[1][:], ACT.Copy).then_inc(u_ready, 1)
                split_hi(2 * i + 1, 1)
                act.wait_ge(mix_done, 2 * g + 1)
                act.wait_ge(pool_dd, 2 * g + 2)
                act.activation(m_hi[:, 0:T], Q, ACT.Copy).then_inc(dhi_ready, 1)
                act.wait_ge(unit_done, 4 * i + 3)
                if first:
                    act.wait_ge(gate_ready, HEADS)
                else:
                    act.wait_ge(pgate_ready, 2 * g)
                act.activation(SIG[:], PJ[0][:], ACT.Sigmoid).then_inc(psig_ready, 1)
                split_hi(2 * i + 2, 0)

            group(0, first=True)
            with act.Fori(1, GROUPS) as g:
                group(g)

            def y_hi(o, j, slot):
                act.wait_ge(consts, N_CONSTS)
                if not (isinstance(j, int) and o == 0 and j < 2):
                    act.wait_ge(unit_done, UNITS + SLOTS * o + j - 1)
                act.activation(m_hi[:, slot * HALF:(slot + 1) * HALF].rearrange("p (a n) -> p a n", a=1),
                               Y[:, ds(j, 1), o * HALF:(o + 1) * HALF], ACT.Copy).then_inc(yhi_ready, 1)

            def out_pair(o, j):
                y_hi(o, 2 * j, 0)
                split_hi((UNITS + SLOTS * o) // 2 + j, 1)
                y_hi(o, 2 * j + 1, 1)
                split_hi((UNITS + SLOTS * o) // 2 + j + 1, 0)

            def tile_rms(n):
                act.wait_ge(res_ready, n + 1)
                if n:
                    act.wait_ge(fss_ready, n)
                act.activation(X1[:], RES[n % OT], ACT.Square, accum_out=ss[:, n:n + 1]).then_inc(fss_ready, 1)
                act.wait_ge(fss_ready, n + 1)
                act.activation(rms[:, n:n + 1], ss[:, n:n + 1], ACT.Sqrt, bias=eps[:, 0:1],
                               scale=1.0 / D).then_inc(frms_ready, 1)

            act.wait_ge(mix_done, 2 * GROUPS)
            for o in range(OG):
                if o == 0:
                    y_hi(0, 0, 0)
                    y_hi(0, 1, 1)
                    second_gate(GROUPS - 1)
                    split_hi(UNITS // 2, 1)
                    split_hi(UNITS // 2 + 1, 0)
                    act.wait_ge(py_ready, PT * GROUPS)
                else:
                    y_hi(o, 0, 0)
                    split_hi((UNITS + SLOTS * o) // 2, 1)
                    y_hi(o, 1, 1)
                    tile_rms(OT * (o - 1))
                    split_hi((UNITS + SLOTS * o) // 2 + 1, 0)
                    tile_rms(OT * (o - 1) + 1)
                    y_hi(o, 2, 0)
                    split_hi((UNITS + SLOTS * o) // 2 + 1, 1)
                    tile_rms(OT * (o - 1) + 2)
                    y_hi(o, 3, 1)
                    split_hi((UNITS + SLOTS * o) // 2 + 2, 0)
                    tile_rms(OT * (o - 1) + 3)
                with act.Fori(1 if o == 0 else 2, SLOTS // 2 - 1) as j:
                    out_pair(o, j)
                if o < OG - 1:
                    out_pair(o, SLOTS // 2 - 1)
            y_hi(OG - 1, SLOTS - 2, 0)
            y_hi(OG - 1, SLOTS - 1, 1)
            split_hi((UNITS + SLOTS * OG) // 2 - 1, 1)
            for t in range(OT - 1):
                tile_rms(OT * (OG - 1) + t)
            for h in range(2):
                n = TT - 1 + h
                act.wait_ge(res_ready, n + 1)
                act.wait_ge(fss_ready, n)
                act.activation(X1[:, h * HALF:(h + 1) * HALF], RES[OT - 1][:, h * HALF:(h + 1) * HALF], ACT.Square,
                               accum_out=ss[:, n:n + 1]).then_inc(fss_ready, 1)
            act.wait_ge(fss_ready, TT + 1)
            act.wait_ge(bias_ready, 1)
            act.activation(rms[:, TT - 1:TT], ss[:, TT:TT + 1], ACT.Sqrt, bias=warm[:],
                           scale=1.0 / D).then_inc(frms_ready, 1)

        @block.vector
        def _(dve):
            def split_lo(n, slot):
                dve.wait_ge(whi_ready, n + 1)
                dve.tensor_tensor(w_lo[:, slot, :], w_raw[:, slot, :], w_hi[:, slot, :].bitcast(f32),
                                  ALU.subtract).then_inc(wlo_ready, 1)

            def normalise(t):
                xt = Y[:, SLOTS - TT + t, :]
                dve.wait_ge(rms_ready, t + 2)
                dve.reciprocal(rin[:, t:t + 1], rms[:, t:t + 1]).then_inc(rin_ready, 1)
                dve.wait_ge(rin_ready, t + 1)
                dve.scalar_tensor_tensor(out=xt, in0=xt, scalar=rin[:, t:t + 1], in1=S[:],
                                         op0=ALU.mult, op1=ALU.mult).then_inc(xn_ready, 1)

            def low_h(t):
                dve.wait_ge(hhi_ready, t + 1)
                cols = slice(t * P, (t + 1) * P)
                dve.tensor_tensor(h_lo[:, :, cols], XT[t % 2][:].rearrange("p (k n) -> p k n", n=P),
                                  h_hi[:, :, cols].bitcast(f32), ALU.subtract).then_inc(hlo_ready, 1)

            dve.wait_ge(grow_loaded, 16)
            normalise(0)
            normalise(1)
            for t in range(TT):
                low_h(t)
                if t + 2 < TT:
                    normalise(t + 2)
                if t < 2:
                    split_lo(t, t)

            dve.wait_ge(params_loaded, 48)
            dve.tensor_tensor(lbm[:], lbl[:, 0, :], lbl[:, 1, :], ALU.max).then_inc(lb_step, 1)
            dve.wait_ge(lb_step, 1)
            for r in range(2):
                dve.tensor_tensor(lbl[:, r, :], lbl[:, r, :], lbm[:], ALU.subtract).then_inc(lb_step, 1)

            dve.wait_ge(lb_exp, 1)
            dve.tensor_tensor(lbm[:], lbl[:, 0, :], lbl[:, 1, :], ALU.add).then_inc(lb_step, 1)
            dve.wait_ge(lb_step, 4)
            dve.reciprocal(omlb[:], lbm[:]).then_inc(lb_step, 1)
            dve.wait_ge(lb_step, 5)
            dve.tensor_tensor(lb[:], lbl[:, 0, :], omlb[:], ALU.mult).then_inc(lb_step, 1)
            dve.wait_ge(lb_step, 6)
            dve.tensor_scalar(omlb[:], lb[:], -1.0, 1.0, ALU.mult, ALU.add).then_inc(lb_step, 1)
            dve.wait_ge(lb_step, 7)

            def column(b, i):
                return b[:, ds(i, 1)]

            def join_queries(h, m):
                other = seg_total(m).rearrange("p (n two) -> p n two", two=2)[:, :, 0:1]
                dve.tensor_tensor(pair_half(Q, m, 1), pair_half(Q, m, 1),
                                  other.to_broadcast([P, T // (2 * m), m]), ALU.mult).then_inc(tree, 1)

            def join_totals(h, m):
                tot = seg_total(m).rearrange("p (n two) -> p n two", two=2)
                dve.tensor_tensor(seg_total(2 * m), tot[:, :, 0], tot[:, :, 1], ALU.mult).then_inc(tree, 1)

            def join_keys(h, m):
                other = seg_total(m).rearrange("p (n two) -> p n two", two=2)[:, :, 1:2]
                dve.tensor_tensor(pair_half(K, m, 0), pair_half(K, m, 0),
                                  other.to_broadcast([P, T // (2 * m), m]), ALU.mult).then_inc(tree, 1)

            def masked_copy(dst, src, mask):
                dve.copy_predicated(dst, mask.bitcast(u32).to_broadcast(list(dst.shape)), src).then_inc(at_dve, 1)

            def copy_segments(k, m, lo, hi, first):
                dst = AB[:].rearrange("p c (n s m) -> p c n s m", s=4, m=m)[:, :, :, first:4, :]
                src = lv(k)[:, 0:TT * VAR].rearrange("p (c n s m) -> p c n s m", c=TT, s=6, m=m)[:, :, :, lo:hi, :]
                mask = masks[:, k:k + 1, :].rearrange("p a (n s m) -> p a n s m", s=6, m=m)[:, :, :, lo:hi, :]
                masked_copy(dst, src, mask)

            def decayed_queries(h, k, m, between):
                v = QV.rearrange("p (n s m) -> p n s m", s=6, m=m)
                q = Q.rearrange("p (n s m) -> p n s m", s=4, m=m)
                tot = seg_total(m).rearrange("p (n s a) -> p n s a", s=4, a=1)
                dve.tensor_tensor(v[:, :, 3:5, :], q[:, :, 2:4, :],
                                  tot[:, :, 1:3, :].to_broadcast([P, T // (4 * m), 2, m]), ALU.mult).then_inc(qv_dve, 1)
                between()
                dve.wait_ge(qv_dve, 4 * h + 2 * k - 1)
                dve.tensor_tensor(v[:, :, 5:6, :], v[:, :, 4:5, :],
                                  tot[:, :, 1:2, :].to_broadcast([P, T // (4 * m), 1, m]), ALU.mult).then_inc(qv_dve, 1)

            def copy_odd():
                masked_copy(AB[:].rearrange("p c (j two) -> p c j two", two=2)[:, :, :, 1],
                            lv(0)[:, 0:TT * VAR].rearrange("p (c x) -> p c x", x=VAR)[:, :, B:VAR],
                            masks[:, 0:1, B:VAR])

            def two_levels(h, k, m):
                n = TS * h + 4 + 6 * (k - 1)
                a = AD * h + 2 + 3 * (k - 1)
                dve.wait_ge(qv_act, 3 * h + k + 1)
                dve.wait_ge(tree, n)
                join_queries(h, m)
                join_totals(h, m)
                dve.wait_ge(tree, n + 2)
                join_queries(h, 2 * m)
                join_totals(h, 2 * m)
                dve.wait_ge(lvl_done, STAGES * h + k + 1)
                dve.wait_ge(at_dve, a)
                join_keys(h, m)
                copy_segments(k, m, 0, 3, 1)
                dve.wait_ge(tree, n + 5)
                dve.wait_ge(at_dve, a + 1)
                join_keys(h, 2 * m)
                copy_segments(k, m, 3, 5, 2)
                dve.wait_ge(at_dve, a + 2)

            def one_level(h, k, m):
                n = TS * h + 4 + 6 * 2 + 3 * (k - 3)
                dve.wait_ge(lvl_done, STAGES * h + k + 1)
                dve.wait_ge(tree, n)
                join_keys(h, m)
                if k == 4:
                    turn_keys(h, n + 1)
                join_queries(h, m)
                join_totals(h, m)

            def turn_keys(h, joined):
                dve.wait_ge(tree, joined)
                dve.transpose(S[:, 0:T - C], K[:, 0:T - C]).then_inc(kb_ready, 1)
                dve.wait_ge(kb_ready, h + 1)
                dve.wait_ge(v_ready, BM * h + BM)
                for d in range(P // 2, P, B):
                    for s in range(0, C, B):
                        dve.tensor_copy(block_at(X1, s, d, TT - 1), block_at(S, d, s, TT - 1)).then_inc(kd_dve, 1)

            def finish_a(h):
                one_level(h, 4, 64)

            def finish_b(h):
                dve.wait_ge(gsig_ready, h + 1)
                if not (isinstance(h, int) and h == 0):
                    dve.wait_ge(y_ready, h)
                dve.tensor_tensor(GATE, PJ[1][:], SIG[:], ALU.mult).then_inc(gate_ready, 1)
                dve.wait_ge(kv_done, h + 1)
                dve.tensor_copy(S[:, C:2 * C], R[:, 0:C]).then_inc(state, 1)
                for c in range(1, TT - 1):
                    dve.wait_ge(state, (TT - 1) * h + c)
                    o = GOFF[C] + c
                    dve.scalar_tensor_tensor(out=S[:, (c + 1) * C:(c + 2) * C], in0=S[:, c * C:(c + 1) * C],
                                             scalar=G[:, o:o + 1], in1=R[:, c * C:(c + 1) * C],
                                             op0=ALU.mult, op1=ALU.add).then_inc(state, 1)
                dve.wait_ge(sq_ready, h + 1)
                dve.wait_ge(gate_ready, h + 1)
                dve.scalar_tensor_tensor(out=GATE, in0=R[:], scalar=column(rg, h), in1=GATE,
                                         op0=ALU.mult, op1=ALU.mult).then_inc(oy_ready, 1)
                dve.wait_ge(sqhi_ready, h + 1)
                dve.tensor_tensor(m_lo[:, 0:T], X1[:], m_hi[:, 0:T].bitcast(f32), ALU.subtract).then_inc(sqlo_ready, 1)

            def finish_c(h):
                dve.wait_ge(orms_ready, h + 1)
                dve.reciprocal(S, S).then_inc(orin_ready, 1)
                dve.wait_ge(orin_ready, h + 1)
                dve.tensor_tensor(Y[:, ds(h, 1), :].rearrange("p a t -> p (a t)"), GATE, S,
                                  ALU.mult).then_inc(y_ready, 1)

            def head(i, first=False):
                if not first:
                    finish_a(i - 1)
                    split_lo(4 * i + 1, 1)
                    finish_b(i - 1)
                else:
                    split_lo(2, 0)
                dve.wait_ge(fsig_ready, i + 1)
                dve.tensor_scalar(F, F, column(omlb, i), column(lb, i), ALU.mult, ALU.add).then_inc(fk_ready, 1)
                dve.wait_ge(fk_ready, 2 * i + 1)
                dve.tensor_scalar(K, F, -1.0, 1.0, ALU.mult, ALU.add).then_inc(fk_ready, 1)
                if not first:
                    split_lo(4 * i + 2, 0)
                    finish_c(i - 1)
                dve.wait_ge(qsig_ready, i + 1)
                if not first:
                    dve.wait_ge(y_ready, i)
                dve.tensor_tensor(QV.rearrange("p (n x) -> p n x", x=VAR)[:, :, 0:B],
                                  PJ[1][:].rearrange("p (n x) -> p n x", x=B),
                                  SIG[:].rearrange("p (n x) -> p n x", x=B), ALU.mult).then_inc(q_ready, 1)
                if not first:
                    dve.wait_ge(o_done, i)
                dve.wait_ge(q_ready, i + 1)
                dve.tensor_tensor(Q.rearrange("p (n x) -> p n x", x=B),
                                  QV.rearrange("p (n x) -> p n x", x=VAR)[:, :, 0:B],
                                  F.rearrange("p (n x) -> p n x", x=B), ALU.mult).then_inc(tree, 1)
                split_lo(4 * i + 3, 1)
                dve.wait_ge(qv_act, 3 * i + 1)
                dve.wait_ge(tree, TS * i + 1)
                dve.tensor_tensor(pair_half(Q, 1, 1), pair_half(Q, 1, 1), pair_half(F, 1, 0), ALU.mult).then_inc(tree, 1)
                dve.tensor_tensor(seg_total(2), pair_half(F, 1, 0).rearrange("p n m -> p (n m)"),
                                  pair_half(F, 1, 1).rearrange("p n m -> p (n m)"), ALU.mult).then_inc(tree, 1)
                dve.wait_ge(fk_ready, 2 * i + 2)
                dve.wait_ge(lvl_done, STAGES * i + 1)
                dve.tensor_tensor(pair_half(K, 1, 0), pair_half(K, 1, 0), pair_half(F, 1, 1), ALU.mult).then_inc(tree, 1)
                masked_copy(AB[:], lv(0)[:, 0:TT * VAR].rearrange("p (c x) -> p c x", x=VAR)[:, :, 0:B],
                            masks[:, 0:1, 0:B])
                dve.wait_ge(at_dve, AD * i + 1)
                dve.wait_ge(tree, TS * i + 3)
                decayed_queries(i, 1, 2, copy_odd)
                two_levels(i, 1, 2)
                decayed_queries(i, 2, 8, lambda: copy_segments(1, 2, 5, 6, 3))
                dve.wait_ge(unit_done, 4 * i + 3)
                if not first:
                    dve.wait_ge(sqlo_ready, i)
                dve.transpose(X1[:], PJ[0][:]).then_inc(vb_ready, 1)
                two_levels(i, 2, 8)
                split_lo(4 * i + 4, 0)
                copy_segments(2, 8, 5, 6, 3)
                one_level(i, 3, 32)

            dve.wait_ge(consts, N_CONSTS)
            head(0, first=True)
            with dve.Fori(1, HEADS) as i:
                head(i)

            steps = [0]

            def done(ins):
                ins.then_inc(pool_step, 1)
                steps[0] += 1

            def pooled(g, c, u):
                w = 2 << g
                dve.wait_ge(u_ready, 2 * g + c + 1)
                if g or c:
                    dve.wait_ge(dlo_ready, 2 * g + c)
                bufs = [Gp, Qp]
                src = u
                for k in range(g + 1):
                    dst = bufs[k % 2]
                    sh = 1 << k
                    done(dve.tensor_tensor(dst[:, PAD:], src[:, PAD:], src[:, PAD - sh:PAD + T - sh], ALU.add))
                    dve.wait_ge(pool_step, steps[0])
                    src = dst
                n = w - 1
                done(dve.tensor_tensor(fix[:, 0:n], src[:, PAD:PAD + n], rcount[:, 0:n], ALU.mult))
                dve.wait_ge(pool_step, steps[0])
                done(dve.scalar_tensor_tensor(out=Q, in0=src[:, PAD:], scalar=1.0 / w, in1=u[:, PAD:],
                                              op0=ALU.mult, op1=ALU.subtract))
                dve.wait_ge(pool_step, steps[0])
                dve.tensor_tensor(Q[:, 0:n], fix[:, 0:n], u[:, PAD:PAD + n], ALU.subtract).then_inc(pool_dd, 1)

            def low_dd(g, c):
                dve.wait_ge(dhi_ready, 2 * g + c + 1)
                dve.tensor_tensor(m_lo[:, 0:T], Q, m_hi[:, 0:T].bitcast(f32), ALU.subtract).then_inc(dlo_ready, 1)

            def first_out(g):
                dve.wait_ge(mix_done, 2 * g + 2)
                dve.wait_ge(pgate_ready, 2 * g + 1)
                dve.scalar_tensor_tensor(out=Y[:, HEADS + PT * g, :], in0=LV[:], scalar=psc[:, PT * g:PT * g + 1],
                                         in1=GATE, op0=ALU.mult, op1=ALU.mult).then_inc(py_ready, 1)

            def second_out(g):
                dve.wait_ge(psig_ready, 2 * g + 2)
                dve.tensor_tensor(S, PJ[1][:], SIG[:], ALU.mult).then_inc(pgate_ready, 1)
                dve.wait_ge(pgate_ready, 2 * g + 2)
                dve.scalar_tensor_tensor(out=Y[:, HEADS + PT * g + 1, :], in0=R[:],
                                         scalar=psc[:, PT * g + 1:PT * g + 2], in1=S[:],
                                         op0=ALU.mult, op1=ALU.mult).then_inc(py_ready, 1)

            for g in range(GROUPS):
                i = HEADS + g
                if g == 0:
                    finish_a(HEADS - 1)
                    split_lo(4 * i + 1, 1)
                    finish_b(HEADS - 1)
                else:
                    second_out(g - 1)
                    split_lo(4 * i + 1, 1)
                split_lo(4 * i + 2, 0)
                pooled(g, 0, Kp)
                dve.wait_ge(pwhi_ready, g + 1)
                dve.tensor_tensor(m_lo[:, T:], X1[:, 0:2 * PT * P], m_hi[:, T:].bitcast(f32),
                                  ALU.subtract).then_inc(pwlo_ready, 1)
                low_dd(g, 0)
                split_lo(4 * i + 3, 1)
                if g == 0:
                    finish_c(HEADS - 1)
                pooled(g, 1, Fp)
                dve.wait_ge(mix_done, 2 * g + 1)
                low_dd(g, 1)
                dve.wait_ge(psig_ready, 2 * g + 1)
                if g == 0:
                    dve.wait_ge(y_ready, HEADS)
                else:
                    dve.wait_ge(py_ready, 2 * g)
                dve.tensor_tensor(GATE, PJ[0][:], SIG[:], ALU.mult).then_inc(pgate_ready, 1)
                split_lo(4 * i + 4, 0)
                first_out(g)

            def y_lo(o, j, slot):
                cols = slice(slot * HALF, (slot + 1) * HALF)
                dve.wait_ge(yhi_ready, SLOTS * o + j + 1)
                dve.tensor_tensor(m_lo[:, cols].rearrange("p (a n) -> p a n", a=1),
                                  Y[:, ds(j, 1), o * HALF:(o + 1) * HALF],
                                  m_hi[:, cols].bitcast(f32).rearrange("p (a n) -> p a n", a=1),
                                  ALU.subtract).then_inc(ylo_ready, 1)

            def out_pair(o, j):
                n = UNITS + SLOTS * o + 2 * j
                y_lo(o, 2 * j, 0)
                split_lo(n + 1, 1)
                y_lo(o, 2 * j + 1, 1)
                split_lo(n + 2, 0)

            def residual(n):
                t = n % OT
                if t < OT - 1:
                    dve.wait_ge(tile_done, (OT - 1) * (n // OT) + t + 1)
                else:
                    dve.wait_ge(unit_done, UNITS + SLOTS * (n // OT + 1))
                dve.wait_ge(xres_loaded[t], 16 * (n // OT) + 16)
                if n >= OT:
                    dve.wait_ge(early_stored[t], 16 * (n // OT))
                dve.tensor_tensor(RES[t], BANKS[t][:], (Q, K, F, G)[t], ALU.add).then_inc(res_ready, 1)

            def residual_half(h):
                cols = slice(h * HALF, (h + 1) * HALF)
                dve.wait_ge(tile_done, (OT - 1) * OG + h + 1)
                dve.wait_ge(xres_loaded[OT - 1], 16 * OG)
                dve.wait_ge(early_stored[OT - 1], 16 * (OG - 1))
                dve.tensor_tensor(RES[OT - 1][:, cols], BANKS[OT - 1][:, cols], G[:, cols],
                                  ALU.add).then_inc(res_ready, 1)

            def finish_tile(n):
                t = n % OT
                dve.wait_ge(frms_ready, n + 1)
                dve.reciprocal(rin[:, n:n + 1], rms[:, n:n + 1]).then_inc(frin_ready, 1)
                dve.wait_ge(frin_ready, n + 1)
                dve.wait_ge(gfin_loaded, 16)
                dve.scalar_tensor_tensor(out=RES[t], in0=RES[t], scalar=rin[:, n:n + 1], in1=V[:],
                                         op0=ALU.mult, op1=ALU.mult).then_inc(fin_ready, 1)

            for o in range(OG):
                n = UNITS + SLOTS * o
                if o == 0:
                    y_lo(0, 0, 0)
                    y_lo(0, 1, 1)
                    second_out(GROUPS - 1)
                    split_lo(n + 1, 1)
                    split_lo(n + 2, 0)
                else:
                    n0 = OT * (o - 1)
                    y_lo(o, 0, 0)
                    residual(n0)
                    residual(n0 + 1)
                    residual(n0 + 2)
                    split_lo(n + 1, 1)
                    residual(n0 + 3)
                    y_lo(o, 1, 1)
                    split_lo(n + 2, 0)
                    finish_tile(n0)
                    y_lo(o, 2, 0)
                    split_lo(n + 3, 1)
                    finish_tile(n0 + 1)
                    y_lo(o, 3, 1)
                    split_lo(n + 4, 0)
                    finish_tile(n0 + 2)
                    y_lo(o, 4, 0)
                    split_lo(n + 5, 1)
                    finish_tile(n0 + 3)
                    y_lo(o, 5, 1)
                    split_lo(n + 6, 0)
                with dve.Fori(1 if o == 0 else 3, SLOTS // 2 - 1) as j:
                    out_pair(o, j)
                if o < OG - 1:
                    out_pair(o, SLOTS // 2 - 1)
            y_lo(OG - 1, SLOTS - 2, 0)
            y_lo(OG - 1, SLOTS - 1, 1)
            split_lo(UNITS + SLOTS * OG - 1, 1)
            n0 = OT * (OG - 1)
            residual(n0)
            residual(n0 + 1)
            finish_tile(n0)
            residual(n0 + 2)
            finish_tile(n0 + 1)
            residual_half(0)
            residual_half(1)
            dve.wait_ge(fss_ready, TT)
            dve.tensor_scalar(warm[:], ss[:, TT - 1:TT], 1.0 / D, EPS, ALU.mult, ALU.add).then_inc(bias_ready, 1)
            finish_tile(n0 + 2)
            dve.wait_ge(frms_ready, TT)
            dve.reciprocal(rin[:, TT - 1:TT], rms[:, TT - 1:TT]).then_inc(frin_ready, 1)
            dve.wait_ge(frin_ready, TT)
            for h in range(2):
                cols = slice(h * HALF, (h + 1) * HALF)
                dve.scalar_tensor_tensor(out=RES[OT - 1][:, cols], in0=RES[OT - 1][:, cols],
                                         scalar=rin[:, TT - 1:TT], in1=V[:, cols],
                                         op0=ALU.mult, op1=ALU.mult).then_inc(fin_ready, 1)

        @block.tensor
        def _(pe):
            def steps(slot, lo, hi, parts=(0, HALF), width=HALF):
                for k in range(lo, hi):
                    cols = slice(k * P, (k + 1) * P)
                    for a, b, first, last in ((w_hi, h_hi, True, False), (w_hi, h_lo, False, False),
                                              (w_lo, h_hi, False, True)):
                        for t in parts:
                            mm = pe.matmul(PJ[slot][:, t:t + width], a[:, slot, cols], b[:, k, t:t + width],
                                           start=(k == 0 and first), stop=(k == KT - 1 and last),
                                           skip_group_check=True)
                if hi == KT and parts[-1] + width == T:
                    mm.then_inc(unit_done, 1)

            def chunk(b, c):
                return b[:, c * C:(c + 1) * C]

            def stage(h, k):
                if k < 2:
                    if not (isinstance(h, int) and h == 0):
                        pe.wait_ge(orms_ready, h)
                else:
                    pe.wait_ge(at_dve, AD * h + (2, 5, 8)[k - 2])
                if k < 3:
                    pe.wait_ge(qv_act, 3 * h + k + 1)
                    if k:
                        pe.wait_ge(qv_dve, 4 * h + 2 * k)
                else:
                    pe.wait_ge(tree, TS * h + (16, 19)[k - 3])
                for c in range(TT):
                    for s in range(0, C, B):
                        keys = K[:, c * C + s:c * C + s + B]
                        if k < 3:
                            n = (c * C + s) // B * VAR
                            mm = pe.matmul(lv(k)[s:s + B, c * VAR:(c + 1) * VAR], keys, QV[:, n:n + VAR],
                                           start=True, stop=True)
                        else:
                            m = (32, 64)[k - 3]
                            t = s - s % (2 * m)
                            if s - t < m:
                                mm = pe.matmul(lv(k)[s:s + B, c * HC + t // 2:c * HC + t // 2 + m], keys,
                                               Q[:, c * C + t + m:c * C + t + 2 * m], start=True, stop=True)
                mm.then_inc(lvl_done, 1)

            def outer_products(h):
                pe.wait_ge(kd_act, BM // 2 * (h + 1))
                pe.wait_ge(kd_dve, BM // 2 * (h + 1))
                pe.wait_ge(v_ready, BM * h + BM)
                if not (isinstance(h, int) and h == 0):
                    pe.wait_ge(oy_ready, h)
                for c in range(TT - 1):
                    mm = pe.matmul(chunk(R, c), chunk(X1, c), chunk(V, c), start=True, stop=True)
                mm.then_inc(kv_done, 1)

            def readout(h):
                pe.wait_ge(tree, TS * h + TS)
                pe.wait_ge(at_act, AA * h + AA)
                pe.wait_ge(state, (TT - 1) * (h + 1))
                for c in range(TT):
                    mm = pe.matmul(chunk(R, c), chunk(V, c), AT[:, c, :], start=True, stop=(c == 0))
                    if c:
                        mm = pe.matmul(chunk(R, c), chunk(S, c), chunk(Q, c), start=False, stop=True)
                mm.then_inc(o_done, 1)

            def means(h):
                pe.wait_ge(sqlo_ready, h + 1)
                for k in range(NH):
                    tok = slice(k * HALF, (k + 1) * HALF)
                    pe.matmul(LV[:, tok], mean_w[:], m_hi[:, tok], start=True, stop=False)
                    mm = pe.matmul(LV[:, tok], mean_w[:], m_lo[:, tok], start=False, stop=True)
                mm.then_inc(mean_done, 1)

            def x_transposes(t):
                pe.wait_ge(xn_ready, t + 1)
                if t >= 2:
                    pe.wait_ge(hlo_ready, t - 1)
                for k in range(KT):
                    mm = pe.transpose(XT[t % 2][:, k * P:(k + 1) * P],
                                      Y[:, SLOTS - TT + t, k * P:(k + 1) * P], ident[:])
                mm.then_inc(xT_ready, 1)

            def first_units():
                pe.wait_ge(ident_ready, 1)
                x_transposes(0)
                x_transposes(1)
                x_transposes(2)
                for q in range(TT // 2):
                    for slot in range(2):
                        if q == 0:
                            pe.wait_ge(wlo_ready, slot + 1)
                        if slot == 0:
                            pe.wait_ge(hlo_ready, 2 * q + 2)
                        steps(slot, 0, KT, [q * 2 * P], 2 * P)
                        if 2 * q + slot + 3 < TT:
                            x_transposes(2 * q + slot + 3)

            def units_01(i, finished):
                pe.wait_ge(wlo_ready, 4 * i + 1)
                pe.wait_ge(vb_ready, finished + 1)
                steps(0, 0, 4)
                outer_products(finished)
                steps(0, 4, 7)
                readout(finished)
                steps(0, 7, 8)
                pe.wait_ge(wlo_ready, 4 * i + 2)
                pe.wait_ge(gate_ready, finished + 1)
                steps(1, 0, 2)
                means(finished)
                steps(1, 2, 8)

            def head(i, first=False):
                if first:
                    first_units()
                else:
                    units_01(i, i - 1)
                pe.wait_ge(wlo_ready, 4 * i + 3)
                pe.wait_ge(fsig_ready, i + 1)
                steps(0, 0, 4)
                stage(i, 0)
                steps(0, 4, 7)
                stage(i, 1)
                steps(0, 7, 8)
                pe.wait_ge(wlo_ready, 4 * i + 4)
                pe.wait_ge(q_ready, i + 1)
                steps(1, 0, 3)
                stage(i, 2)
                steps(1, 3, 5)
                stage(i, 3)
                steps(1, 5, 7)
                stage(i, 4)
                steps(1, 7, 8)

            head(0, first=True)
            with pe.Fori(1, HEADS) as i:
                head(i)

            def mix(g, c):
                pe.wait_ge(dlo_ready, 2 * g + c + 1)
                if c == 0:
                    pe.wait_ge(pwlo_ready, g + 1)
                for d, dst in enumerate((LV, R)):
                    cols = slice(T + c * PT * P + d * P, T + c * PT * P + (d + 1) * P)
                    for h in range(NH):
                        tok = slice(h * HALF, (h + 1) * HALF)
                        for k, (a, b) in enumerate(((m_hi, m_hi), (m_hi, m_lo), (m_lo, m_hi))):
                            mm = pe.matmul(dst[:, tok], a[:, cols], b[:, tok], start=(c == 0 and k == 0),
                                           stop=(c == PT - 1 and k == 2), skip_group_check=True)
                mm.then_inc(mix_done, 1)

            def group(g, first=False):
                i = g + HEADS
                if first:
                    units_01(i, HEADS - 1)
                else:
                    pe.wait_ge(wlo_ready, 4 * i + 1)
                    pe.wait_ge(pgate_ready, 2 * g - 1)
                    steps(0, 0, KT)
                    pe.wait_ge(wlo_ready, 4 * i + 2)
                    pe.wait_ge(pgate_ready, 2 * g)
                    steps(1, 0, KT)
                pe.wait_ge(wlo_ready, 4 * i + 3)
                pe.wait_ge(u_ready, 2 * g + 1)
                steps(0, 0, 3)
                if first:
                    pe.wait_ge(orms_ready, HEADS)
                    pe.wait_ge(oy_ready, HEADS)
                else:
                    pe.wait_ge(py_ready, 2 * g)
                mix(g, 0)
                steps(0, 3, 8)
                pe.wait_ge(wlo_ready, 4 * i + 4)
                pe.wait_ge(u_ready, 2 * g + 2)
                steps(1, 0, 4)
                mix(g, 1)
                steps(1, 4, 8)

            group(0, first=True)
            with pe.Fori(1, GROUPS) as g:
                group(g)

            def out_tile(t, slot, first, last, halves=range(D // HALF)):
                tok = slice(slot * HALF + t * P, slot * HALF + (t + 1) * P)
                for k, (a, b) in enumerate(((m_hi, w_hi), (m_hi, w_lo), (m_lo, w_hi))):
                    for h in halves:
                        cols = slice(h * HALF, (h + 1) * HALF)
                        mm = pe.matmul(BANKS[t][:, cols], a[:, tok], b[:, slot, cols],
                                       start=(first and k == 0), stop=(last and k == 2),
                                       skip_group_check=True)
                return mm

            def bank_free(o, t):
                if o:
                    pe.wait_ge(res_ready, OT * (o - 1) + t + 1)
                else:
                    pe.wait_ge(*((pgate_ready, 2 * GROUPS - 1), (py_ready, 2 * GROUPS - 1),
                                 (pgate_ready, 2 * GROUPS), (py_ready, 2 * GROUPS))[t])

            def out_unit(o, n, slot, first=False, last=False):
                pe.wait_ge(wlo_ready, n + 1)
                pe.wait_ge(ylo_ready, n - UNITS + 1)
                for t in range(OT):
                    if first:
                        bank_free(o, t)
                    mm = out_tile(t, slot, first, last)
                    if last and t < OT - 1:
                        mm.then_inc(tile_done, 1)
                mm.then_inc(unit_done, 1)

            for o in range(OG):
                n0 = UNITS + SLOTS * o
                out_unit(o, n0, 0, first=True)
                out_unit(o, n0 + 1, 1)
                with pe.Fori(1, SLOTS // 2 - 1) as j:
                    out_unit(o, n0 + 2 * j, 0)
                    out_unit(o, n0 + 2 * j + 1, 1)
                if o < OG - 1:
                    out_unit(o, n0 + SLOTS - 2, 0)
                    out_unit(o, n0 + SLOTS - 1, 1, last=True)
            pe.wait_ge(wlo_ready, UNITS + SLOTS * OG - 1)
            pe.wait_ge(ylo_ready, SLOTS * OG - 1)
            for t in range(2):
                out_tile(t, 0, False, False)
            pe.wait_ge(wlo_ready, UNITS + SLOTS * OG)
            pe.wait_ge(ylo_ready, SLOTS * OG)
            for t in range(2):
                out_tile(t, 1, False, True).then_inc(tile_done, 1)
            for t in range(2, OT - 1):
                out_tile(t, 0, False, False)
                out_tile(t, 1, False, True).then_inc(tile_done, 1)
            for h in range(D // HALF):
                out_tile(OT - 1, 0, False, False, [h])
                out_tile(OT - 1, 1, False, True, [h]).then_inc(tile_done, 1)


_INS = ['x', 'norm1_g', 'w_in', 'pool_w', 'pool_scale', 'lb_logits', 'rec_norm_g', 'w_out', 'final_norm_g']


def kernel(**inputs):
    import numpy as _np
    import concourse.bacc as _bacc
    from concourse import mybir as _mybir
    from concourse.bass_utils import run_bass_kernel_spmd as _run

    nc = _bacc.Bacc("TRN2", target_bir_lowering=False, num_devices=1)
    arrays, args = {}, []
    for name in _INS:
        a = _np.ascontiguousarray(inputs[name])
        arrays[f"in_{name}_dram"] = a
        args.append(nc.dram_tensor(f"in_{name}_dram", a.shape, _mybir.dt.from_np(a.dtype), kind="ExternalInput").ap())
    shape = inputs["x"].shape
    args.append(nc.dram_tensor("out_0_dram", shape, _mybir.dt.float32, kind="ExternalOutput").ap())
    hybrid_pool_hgrn2_kernel(nc, *args)
    r = _run(nc, [arrays], core_ids=[0])
    return r.results[0]["out_0_dram"]
```
